# Optimizing a Trainium2 kernel written in Bass

```python
import math
import jax, jax.numpy as jnp
from jax import lax
import numpy as np

D_MODEL = 1024
BATCH = 1
SEQ = 1024
DEPTH = 1

HEAD_DIM = 64
DIL_GROUPS = ((128, 1), (512, 4), (2048, 16))
A_HEADS_PER_GROUP = 4
A_HEADS = A_HEADS_PER_GROUP * len(DIL_GROUPS)
A_OUT = A_HEADS_PER_GROUP * HEAD_DIM
B_Q_HEADS = 8
B_KV_HEADS = 2
B_WINDOW = 128
B_OUT = B_Q_HEADS * HEAD_DIM
BLOCK = 128
N_BUCKETS = 32
MAX_DISTANCE = 2048
TOTAL_HEADS = A_HEADS + B_Q_HEADS
D_FF = 2816
EPS = 1e-6
A_QKV_W = A_HEADS * HEAD_DIM
B_KV_W = B_KV_HEADS * HEAD_DIM
SPLITS = (A_QKV_W, A_QKV_W, A_QKV_W, B_OUT, B_KV_W, B_KV_W, D_MODEL, D_MODEL)
D_IN = sum(SPLITS)

kernel_name = "hybrid_dilated_swa_sink_macaron"

def rms_norm(x, g):
    x32 = x.astype(jnp.float32)
    y = x32 * lax.rsqrt(jnp.mean(x32 * x32, axis=-1, keepdims=True) + EPS)
    return (y * g.astype(jnp.float32)).astype(x.dtype)

def swiglu(x, w_gate, w_up, w_down):
    return (jax.nn.silu(x @ w_gate) * (x @ w_up)) @ w_down

def t5_bucket(dist):
    max_exact = N_BUCKETS // 2
    n = jnp.maximum(dist, 0)
    nf = jnp.maximum(n, 1).astype(jnp.float32)
    large = max_exact + (jnp.log(nf / max_exact) / math.log(MAX_DISTANCE / max_exact)
                         * (N_BUCKETS - max_exact)).astype(jnp.int32)
    large = jnp.minimum(large, N_BUCKETS - 1)
    return jnp.where(n < max_exact, n, large)

def band_geometry(max_steps):
    qi = jnp.arange(BLOCK)[:, None]
    ki = jnp.arange(2 * BLOCK)[None, :]
    dist = qi + BLOCK - ki
    band = (dist >= 0) & (dist <= max_steps)
    return dist, band

def rel_bias_block(table, dist, stride, h0, h1):
    b = table[t5_bucket(dist * stride)][..., h0:h1]
    return jnp.transpose(b, (2, 0, 1))

def banded_attention(q, k, v, bias, max_steps, sinks=None):
    N, L, H, hd = q.shape
    hkv = k.shape[2]
    g = H // hkv
    nb = -(-L // BLOCK)
    lp = nb * BLOCK
    pad = ((0, 0), (0, lp - L), (0, 0), (0, 0))
    qb = jnp.pad(q, pad).reshape(N, nb, BLOCK, hkv, g, hd)
    kb = jnp.pad(k, pad).reshape(N, nb, BLOCK, hkv, hd)
    vb = jnp.pad(v, pad).reshape(N, nb, BLOCK, hkv, hd)

    def with_prev(t):
        prev = jnp.pad(t, ((0, 0), (1, 0), (0, 0), (0, 0), (0, 0)))[:, :-1]
        return jnp.concatenate([prev, t], axis=2)

    kc, vc = with_prev(kb), with_prev(vb)
    _, band = band_geometry(max_steps)
    first = (jnp.arange(nb) == 0)[:, None, None]
    before_start = (jnp.arange(2 * BLOCK) < BLOCK)[None, None, :]
    valid = band[None] & ~(first & before_start)

    logits = jnp.einsum('nbqhgd,nbkhd->nbhgqk', qb, kc).astype(jnp.float32) * (hd ** -0.5)
    logits = logits + bias.astype(jnp.float32).reshape(hkv, g, BLOCK, 2 * BLOCK)
    logits = jnp.where(valid[None, :, None, None], logits, -jnp.inf)
    m = jnp.max(logits, axis=-1)
    if sinks is not None:
        s = sinks.astype(jnp.float32).reshape(hkv, g)[:, :, None]
        m = jnp.maximum(m, s)
    p = jnp.exp(logits - m[..., None])
    denom = jnp.sum(p, axis=-1)
    if sinks is not None:
        denom = denom + jnp.exp(s - m)
    out = jnp.einsum('nbhgqk,nbkhd->nbqhgd', p.astype(vc.dtype), vc)
    out = (out / jnp.transpose(denom, (0, 1, 4, 2, 3))[..., None]).astype(q.dtype)
    out = out.reshape(N, lp, H, hd)[:, :L]
    lse = jnp.transpose(m + jnp.log(denom), (0, 1, 4, 2, 3)).reshape(N, lp, H)[:, :L]
    return out, lse

def fold_residues(t, d):
    B, S, H, hd = t.shape
    t = t.reshape(B, S // d, d, H, hd)
    return jnp.transpose(t, (0, 2, 1, 3, 4)).reshape(B * d, S // d, H, hd)

def unfold_residues(t, B, d):
    Bd, Ld = t.shape[:2]
    rest = t.shape[2:]
    t = t.reshape((B, d, Ld) + rest)
    perm = (0, 2, 1) + tuple(range(3, t.ndim))
    return jnp.transpose(t, perm).reshape((B, d * Ld) + rest)

def dilated_attention(q, k, v, table):
    B, S = q.shape[:2]
    outs, lses = [], []
    for gi, (window, d) in enumerate(DIL_GROUPS):
        h0, h1 = gi * A_HEADS_PER_GROUP, (gi + 1) * A_HEADS_PER_GROUP
        steps = window // d
        dist, _ = band_geometry(steps)
        bias = rel_bias_block(table, dist, d, h0, h1)
        o, lse = banded_attention(fold_residues(q[:, :, h0:h1], d), fold_residues(k[:, :, h0:h1], d),
                                  fold_residues(v[:, :, h0:h1], d), bias, steps)
        outs.append(unfold_residues(o, B, d))
        lses.append(unfold_residues(lse, B, d))
    alpha = jax.nn.softmax(jnp.stack(lses, axis=0), axis=0)
    y = jnp.sum(alpha[..., None] * jnp.stack(outs, axis=0).astype(jnp.float32), axis=0)
    return y.reshape(B, S, A_OUT).astype(q.dtype)

def sliding_window_sink_attention(q, k, v, sinks, table):
    B, S = q.shape[:2]
    dist, _ = band_geometry(B_WINDOW - 1)
    bias = rel_bias_block(table, dist, 1, A_HEADS, TOTAL_HEADS)
    o, _ = banded_attention(q, k, v, bias, B_WINDOW - 1, sinks)
    return o.reshape(B, S, B_OUT)

def hybrid_layer(x, ffn1_norm, ffn1_w_gate, ffn1_w_up, ffn1_w_down, mix_norm, w_in, b_in,
                 w_branch_a, w_branch_b, w_out, sinks, rel_bias,
                 ffn2_norm, ffn2_w_gate, ffn2_w_up, ffn2_w_down):
    B, S, _ = x.shape
    h = x + 0.5 * swiglu(rms_norm(x, ffn1_norm), ffn1_w_gate, ffn1_w_up, ffn1_w_down)
    u = rms_norm(h, mix_norm)
    z = u @ w_in + b_in
    aq, ak, av, bq, bk, bv, ga, gb = jnp.split(z, np.cumsum(SPLITS)[:-1].tolist(), axis=-1)
    heads = lambda t: t.reshape(B, S, -1, HEAD_DIM)
    ya = dilated_attention(heads(aq), heads(ak), heads(av), rel_bias)
    yb = sliding_window_sink_attention(heads(bq), heads(bk), heads(bv), sinks, rel_bias)
    merged = jax.nn.sigmoid(ga) * (ya @ w_branch_a) + jax.nn.sigmoid(gb) * (yb @ w_branch_b)
    h = h + merged @ w_out
    h = h + 0.5 * swiglu(rms_norm(h, ffn2_norm), ffn2_w_gate, ffn2_w_up, ffn2_w_down)
    return h

def setup_inputs(seed: int = 0) -> dict:
    key = jax.random.key(seed)
    ks = jax.random.split(key, 20)
    L = DEPTH

    def w(k, shape, fan_in):
        return jax.random.normal(k, shape, jnp.float32) * (fan_in ** -0.5)

    def gain(k, shape):
        return 1.0 + 0.01 * jax.random.normal(k, shape, jnp.float32)

    return {
        "x": jax.random.normal(ks[0], (BATCH, SEQ, D_MODEL), jnp.float32),
        "ffn1_norm": gain(ks[1], (L, D_MODEL)),
        "ffn1_w_gate": w(ks[2], (L, D_MODEL, D_FF), D_MODEL),
        "ffn1_w_up": w(ks[3], (L, D_MODEL, D_FF), D_MODEL),
        "ffn1_w_down": w(ks[4], (L, D_FF, D_MODEL), D_FF),
        "mix_norm": gain(ks[5], (L, D_MODEL)),
        "w_in": w(ks[6], (L, D_MODEL, D_IN), D_MODEL),
        "b_in": 0.01 * jax.random.normal(ks[7], (L, D_IN), jnp.float32),
        "w_branch_a": w(ks[8], (L, A_OUT, D_MODEL), A_OUT),
        "w_branch_b": w(ks[9], (L, B_OUT, D_MODEL), B_OUT),
        "w_out": w(ks[10], (L, D_MODEL, D_MODEL), D_MODEL),
        "sinks": 0.5 * jax.random.normal(ks[11], (L, B_Q_HEADS), jnp.float32),
        "rel_bias": 0.5 * jax.random.normal(ks[12], (N_BUCKETS, TOTAL_HEADS), jnp.float32),
        "ffn2_norm": gain(ks[13], (L, D_MODEL)),
        "ffn2_w_gate": w(ks[14], (L, D_MODEL, D_FF), D_MODEL),
        "ffn2_w_up": w(ks[15], (L, D_MODEL, D_FF), D_MODEL),
        "ffn2_w_down": w(ks[16], (L, D_FF, D_MODEL), D_FF),
        "final_norm": gain(ks[17], (D_MODEL,)),
    }

def reference(x, ffn1_norm, ffn1_w_gate, ffn1_w_up, ffn1_w_down, mix_norm, w_in, b_in,
              w_branch_a, w_branch_b, w_out, sinks, rel_bias,
              ffn2_norm, ffn2_w_gate, ffn2_w_up, ffn2_w_down, final_norm):
    h = x
    for l in range(DEPTH):
        h = hybrid_layer(h, ffn1_norm[l], ffn1_w_gate[l], ffn1_w_up[l], ffn1_w_down[l], mix_norm[l],
                         w_in[l], b_in[l], w_branch_a[l], w_branch_b[l], w_out[l], sinks[l], rel_bias,
                         ffn2_norm[l], ffn2_w_gate[l], ffn2_w_up[l], ffn2_w_down[l])
    return rms_norm(h, final_norm)


_drawn_inputs = setup_inputs


def setup_inputs(seed=0):
    import zlib

    import numpy as np

    out = dict(_drawn_inputs(seed))
    spreads = {}
    factors = {'ffn1_norm': 8.0,
     'mix_norm': 8.0,
     'b_in': 8.0,
     'sinks': 200.0,
     'ffn2_norm': 171.894,
     'final_norm': 189.518,
     'rel_bias': 2.908}
    for name, (base, spread) in spreads.items():
        noise = np.random.default_rng([zlib.crc32(name.encode()), seed]).standard_normal(out[name].shape)
        drawn = base * np.exp(spread * noise) if base else spread * noise
        out[name] = __import__('jax').numpy.asarray(drawn.astype(out[name].dtype))
    for name, factor in factors.items():
        out[name] = (out[name] * factor).astype(out[name].dtype)
    return out
```

```python
import math
from contextlib import ExitStack

import numpy as np

import concourse.bass as bass
from concourse import mybir

P = 128
D_MODEL, SEQ, D_FF = 1024, 1024, 2816
HD = 64
EPS = 1e-6
DILATIONS = (1, 4, 16)
WINDOWS = (128, 512, 2048)
A_SLOTS = 4
A_HEADS, B_HEADS, B_KV = 12, 8, 2
B_WINDOW = 128
N_BUCKETS, MAX_DISTANCE = 32, 2048
HEADS = A_HEADS + B_HEADS
D_IN = 3 * A_HEADS * HD + B_HEADS * HD + 2 * B_KV * HD + 2 * D_MODEL

KT = D_MODEL // P
HALF = SEQ // 2
FT = D_FF // P
FFN_STEPS = FT // 2
UNIT = 1024
FFN_UNITS = 6
A_UNITS = 6
B_UNITS = 4
HEAD_UNITS = A_UNITS + B_UNITS
PROJ = 3 * A_UNITS + 2 + B_UNITS
MERGE_STEPS = KT // 2
MERGE_UNITS = 8
PROJ_0 = FFN_UNITS * FFN_STEPS
MERGE_0 = PROJ_0 + PROJ
FFN2_0 = MERGE_0 + MERGE_UNITS * MERGE_STEPS
N_UNITS = FFN2_0 + FFN_UNITS * FFN_STEPS
RING = 4
CHUNKS = 4 * HEAD_UNITS
QT = SEQ // P
BIN_TILES = D_IN // P
NEG = -1e30
VEC = 384



def unit_of(u):
    return ("A", u // 3, u % 3) if u < A_UNITS else ("B", u - A_UNITS, 0)


def proj_tiles():
    out = []
    for u in range(A_UNITS + 1):
        out += [("q", u), ("k", u), ("v", u)]
    return out + [("q", u) for u in range(A_UNITS + 1, HEAD_UNITS)]


def head_columns(role, u):
    kind, a, g = unit_of(u)
    qa, qb = 0, 3 * A_HEADS * HD
    if kind == "A":
        at = {"q": 0, "k": 1, "v": 2}[role] * A_HEADS * HD + (A_SLOTS * g + 2 * a) * HD
        return np.arange(at, at + P)
    if role == "q":
        return np.concatenate([np.arange(qb + h * HD, qb + (h + 1) * HD) for h in (a, a + B_HEADS // 2)])
    at = qb + B_HEADS * HD + (0 if role == "k" else B_KV * HD)
    return np.arange(at, at + P)


def bucket(dist):
    max_exact = N_BUCKETS // 2
    n = np.maximum(dist, 0)
    nf = np.maximum(n, 1).astype(np.float32)
    large = max_exact + (np.log(nf / np.float32(max_exact)) / np.float32(math.log(MAX_DISTANCE / max_exact))
                         * np.float32(N_BUCKETS - max_exact)).astype(np.int32)
    return np.where(n < max_exact, n, np.minimum(large, N_BUCKETS - 1))


def distance_onehot():
    out = np.zeros((N_BUCKETS + 1, 4, VEC), np.float32)
    steps = [(d, w // d) for w, d in zip(WINDOWS, DILATIONS)] + [(1, B_WINDOW - 1)]
    for v, (d, most) in enumerate(steps):
        for j in range(VEC):
            dist = 2 * P - 1 - j
            row = int(bucket(np.array(dist * d))) if 0 <= dist <= most else N_BUCKETS
            out[row, v, j] = 1.0
    return out


JOBS = [(n, hf) for hf in range(2) for n in range(2)] + [(n, hf) for n in range(2, PROJ) for hf in range(2)]
JOB_INDEX = {job: j for j, job in enumerate(JOBS)}


def attention_plan():
    plan = []
    jobs = iter(range(2 * PROJ))

    def job(n=1):
        for _ in range(n):
            plan.append(("job", next(jobs)))

    job(2)
    plan.append(("ssq",))
    job(2)
    for i in range(HEADS // 2):
        plan.append(("m", "bias", i))
        if i in (3, 7):
            job()
    plan.append(("m", "v", 0, 0))
    for u in range(HEAD_UNITS + 1):
        for s in range(4):
            c = 4 * u + s
            if c < CHUNKS:
                plan.append(("qk", c))
            n_jobs = (1, 2, 1, 2)[s] if u < A_UNITS else (0, 1, 0, 1)[s] if u < HEAD_UNITS - 1 else 0
            if n_jobs:
                job()
            if s == 0 and u <= A_UNITS:
                plan.append(("m", "v", u, 1))
            if s == 2 and u:
                plan.append(("m", "o", u - 1, 0))
            if s == 3 and u:
                plan.append(("m", "o", u - 1, 1))
            pair = {4: 0, 7: 1}.get(u)
            if s == 3 and u in (3, 6):
                plan.append(("m", "stat", u // 3 - 1))
            if pair is not None and s < 2:
                plan += [("m", "lse", pair, s, g) for g in range(3)]
            if 0 <= c - 1 < CHUNKS:
                plan.append(("t", c - 1))
            if 0 <= c - 2 < CHUNKS:
                plan.append(("pv", c - 2))
            if n_jobs == 2:
                job()
            if s == 3 and u < A_UNITS:
                plan.append(("m", "v", u + 1, 0))
    assert next(jobs, None) is None
    return plan


PLAN = attention_plan()
M_EVENTS = [e for e in PLAN if e[0] == "m"]
M_INDEX = {e: n for n, e in enumerate(M_EVENTS)}


def build(nc, xT, stream, gains, b_in, sinks, rel_bias, onehot, bias_rows, h_spill, outT):
    f32, f32r = mybir.dt.float32, mybir.dt.float32r
    ALU = mybir.AluOpType
    ACT = mybir.ActivationFunctionType

    BASE = 16512
    K = 1024
    names = iter(range(1000))

    def place(name, shape, offset, dtype=f32):
        return nc.alloc_sbuf_tensor_at(f"{name}_{next(names)}", shape, dtype, offset=BASE + offset)

    ident = place("ident", [P, P], 0)
    ones = place("ones", [P, P], 512)
    bias_in = place("bias_in", [P, BIN_TILES], 1024)
    bias_q = place("bias_q", [P, BIN_TILES], 1184)
    gain = place("gain", [P, 4, KT], 1344)
    sink = place("sink", [P, B_HEADS], 1472)
    eps = place("eps", [P, 1], 1504)
    gate_bias = place("gate_bias", [P, 4], 1536)
    R = 1568

    def at(k):
        return R + int(k * K)

    h = place("h", [P, KT, SEQ], at(0))
    xh = place("xh", [P, KT, SEQ], at(32), f32r)
    xl = place("xl", [P, KT, SEQ], at(64), f32r)
    wh = [place(f"wh{s}", [P, UNIT], at(96 + 8 * s), f32r) for s in range(FFN_UNITS)]
    wl = [place(f"wl{s}", [P, UNIT], at(100 + 8 * s), f32r) for s in range(FFN_UNITS)]
    raw = [place(f"raw{s}", [P, UNIT], at(144 + 4 * s)) for s in range(2)]
    gh = place("gh", [P, 2, SEQ], at(152), f32r)
    gl = place("gl", [P, 2, SEQ], at(160), f32r)
    tmp = [place(f"tmp{s}", [P, HALF], at(168 + 2 * s)) for s in range(4)]
    skew = place("skew", [P, HEADS, 2 * P], at(176))
    flip = place("flip", [P, P], at(196))
    tab = place("tab", [N_BUCKETS + 1, HEADS], at(152))
    hot = place("hot", [N_BUCKETS + 1, 4, VEC], at(153))
    rows = place("rows", [B_HEADS, 4, VEC], at(160))
    qs = [place("q0", [P, SEQ], at(0)), place("q1", [P, SEQ], at(4))]
    ks = [place("k0", [P, SEQ], at(8)), place("k1", [P, SEQ], at(190))]
    vs = [place("v0", [P, QT, P], at(12)), place("v1", [P, QT, P], at(194))]
    vt = place("vt", [P, SEQ], at(16))
    ob = place("ob", [P, QT, P], at(20))
    sp = [place(f"sp{s}", [P, 4, 2 * P], at(24 + 4 * s)) for s in range(2)]
    bias_B = place("bias_B", [P, B_HEADS, 2 * P], at(152))
    pt = [place(f"pt{s}", [P, 4, 2 * P], at(160 + 4 * s)) for s in range(2)]
    bias_2 = place("bias_2", [P, A_SLOTS, P], at(168))
    negm = place("negm", [P, 4 * CHUNKS], at(170))
    den = place("den", [P, 4 * CHUNKS], at(170) + 640)
    sexp = place("sexp", [P, 4 * 4 * B_UNITS], at(170) + 1280)
    lse = place("lse", [P, 3, 16], at(170) + 1536)
    rmax = place("rmax", [P, 2, 4], at(170) + 1728)
    rden = place("rden", [P, 2, 4], at(170) + 1760)
    lseT = place("lseT", [16, 3, P], at(170) + 2048)
    bias_A = place("bias_A", [P, 2 * A_SLOTS, 2 * P], at(198))
    Y = [174 + 4 * n for n in range(8)] + [128 + 4 * n for n in range(4)]
    yah = [place(f"yah{p}", [P, SEQ], at(Y[2 * p]), f32r) for p in range(2)]
    yal = [place(f"yal{p}", [P, SEQ], at(Y[2 * p + 1]), f32r) for p in range(2)]
    og = [place(f"og{g}", [P, SEQ], at(Y[8 + g])) for g in range(3)]
    sel = place("sel", [16, QT, P], at(Y[11]))
    YB = (8, 10, 4, 6)
    ybh = [place(f"ybh{i}", [P, SEQ], at(Y[YB[i]]), f32r) for i in range(B_UNITS)]
    ybl = [place(f"ybl{i}", [P, SEQ], at(Y[YB[i] + 1]), f32r) for i in range(B_UNITS)]
    mix = [[place(f"mix{p}{n}", [P, HALF], at(Y[(2, 4)[p]] + 2 * n)) for n in range(4)] for p in range(2)]

    ctx = ExitStack()
    with ctx:
        bank = [ctx.enter_context(nc.psum_tensor(f"bank{n}", [P, HALF], f32)) for n in range(8)]

        def sem(name):
            return ctx.enter_context(nc.semaphore(name))

        x_in = [sem("x_in0"), sem("x_in1")]
        const_in = sem("const_in")
        tab_in = sem("tab_in")
        raw_in = [sem("raw_in0"), sem("raw_in1")]
        rows_out = sem("rows_out")
        skew_in = sem("skew_in")
        spilled = sem("spilled")
        h_back = sem("h_back")
        stored = sem("stored")
        made = sem("made")
        bias_scaled = sem("bias_scaled")
        sel_made = sem("sel_made")
        vec_done = sem("vec_done")
        vec_out = sem("vec_out")
        w_high = sem("w_high")
        w_low = sem("w_low")
        sq_done = sem("sq_done")
        sq_sum = sem("sq_sum")
        ssq = sem("ssq")
        root = sem("root")
        rstd_done = sem("rstd_done")
        x_scaled = sem("x_scaled")
        x_high = sem("x_high")
        x_low = sem("x_low")
        gu_done = sem("gu_done")
        silu_done = sem("silu_done")
        prod_done = sem("prod_done")
        g_high = sem("g_high")
        g_low = sem("g_low")
        down_done = sem("down_done")
        down_added = sem("down_added")
        job_done = sem("job_done")
        job_out = sem("job_out")
        qk_done = sem("qk_done")
        max_done = sem("max_done")
        negm_done = sem("negm_done")
        exp_done = sem("exp_done")
        t_done = sem("t_done")
        t_out = sem("t_out")
        pv_done = sem("pv_done")
        den_done = sem("den_done")
        pv_out = sem("pv_out")
        m_done = sem("m_done")
        m_out = sem("m_out")
        mask_set = sem("mask_set")
        yb_high = sem("yb_high")
        ln_done = sem("ln_done")
        lse_made = sem("lse_made")
        mix_step = sem("mix_step")
        mix_exp = sem("mix_exp")
        ya_high = sem("ya_high")
        y_low = sem("y_low")
        part_done = sem("part_done")
        gate_bias_set = sem("gate_bias_set")
        sig_done = sem("sig_done")
        mul_done = sem("mul_done")
        m_high = sem("m_high")
        m_low = sem("m_low")

        block = ctx.enter_context(nc.Block())

        def fold(buf, g, hf):
            if g == 0:
                return buf[:, hf * HALF:(hf + 1) * HALF]
            d = DILATIONS[g]
            n = HALF // d
            return buf[:, :].rearrange("p (r b q) -> p q r b", r=d, b=2)[:, 0:n, :, hf]

        def unfold(buf, g, hf):
            if g == 0:
                return buf[:, hf * HALF:(hf + 1) * HALF]
            if g == 1:
                return buf[:, :].rearrange("p (b q r) -> p r b q", b=2, r=4)[:, 2 * hf:2 * hf + 2]
            return buf[:, :].rearrange("p (j r) -> p r j", r=16)[:, 8 * hf:8 * hf + 8]

        def has_previous(u, tile):
            kind, _, g = unit_of(u)
            return tile > 0 if g == 0 else g == 1 and tile % 2 == 1

        DOWN_MERGE = 16 * FFN_STEPS
        DOWN_FFN2 = DOWN_MERGE + 16 * MERGE_STEPS

        @block.sync
        def _(sp_):
            for hf in range(2):
                cols = slice(hf * HALF, (hf + 1) * HALF)
                sp_.dma_start(h[:, :, cols], xT.rearrange("(k p) t -> p k t", p=P)[:, :, cols]).then_inc(x_in[hf], 16)
                sp_.dma_start(raw[hf][:], stream[hf]).then_inc(raw_in[hf], 16)
            with sp_.Fori(1, N_UNITS // 2) as n:
                for s in range(2):
                    sp_.wait_ge(w_low, 2 * n - 1 + s)
                    sp_.dma_start(raw[s][:], stream[2 * n + s]).then_inc(raw_in[s], 16)
            for hf in range(2):
                for k in range(KT):
                    cols = slice(hf * HALF, (hf + 1) * HALF)
                    sp_.wait_ge(x_scaled, 48 + 8 * hf + k + 1)
                    sp_.dma_start(outT[k * P:(k + 1) * P, cols], h[:, k, cols]).then_inc(stored, 16)
            sp_.wait_ge(stored, 16 * 16)

        @block.gpsimd
        def _(pool):
            nc.gpsimd.memset(eps[:], EPS).then_inc(made, 1)
            nc.gpsimd.memset(ones[:], 1.0).then_inc(made, 1)
            nc.gpsimd.memset(ident[:], 0.0).then_inc(made, 1)
            nc.gpsimd.memset(flip[:], 0.0).then_inc(made, 1)
            pool.wait_ge(made, 4)
            nc.gpsimd.memset(tab[N_BUCKETS:, :], NEG).then_inc(made, 1)
            pool.wait_ge(made, 5)
            nc.gpsimd.affine_select(out=ident[:], in_=ident[:], compare_op=ALU.not_equal, fill=1.0, base=0,
                                    pattern=[[-1, P]], channel_multiplier=1).then_inc(made, 1)
            nc.gpsimd.affine_select(out=flip[:], in_=flip[:], compare_op=ALU.not_equal, fill=1.0,
                                    base=1 - P, pattern=[[1, P]], channel_multiplier=1).then_inc(made, 1)
            pool.wait_ge(vec_out, 4)
            for v, (first, n) in enumerate(((0, 4), (4, 4), (8, 4), (12, 8))):
                pool.dma_start(bias_rows[first:first + n, :], rows[0:n, v, :]).then_inc(rows_out, 16)
            pool.wait_ge(rows_out, 64)
            pool.dma_start(skew[:], bass.AP(tensor=bias_rows.tensor, offset=bias_rows.offset,
                                            ap=[[1, P], [VEC, HEADS], [1, 2 * P]])).then_inc(skew_in, 16)
            for hf in range(2):
                for k in range(KT):
                    cols = slice(hf * HALF, (hf + 1) * HALF)
                    pool.wait_ge(down_added, DOWN_MERGE - 16 + 8 * hf + k + 1)
                    pool.dma_start(h_spill[:, k, cols], h[:, k, cols]).then_inc(spilled, 16)
            pool.wait_ge(down_done, DOWN_MERGE)
            nc.gpsimd.memset(sel[:], 0.0).then_inc(sel_made, 1)
            pool.wait_ge(sel_made, 1)
            nc.gpsimd.affine_select(out=sel[:].rearrange("k t (s c) -> k t s c", s=2),
                                    in_=sel[:].rearrange("k t (s c) -> k t s c", s=2),
                                    compare_op=ALU.not_equal, fill=1.0, base=0,
                                    pattern=[[-1, QT], [-QT, 2], [0, HD]], channel_multiplier=1).then_inc(sel_made, 1)
            pool.wait_ge(spilled, 16 * 16)
            pool.wait_ge(m_out, len(M_EVENTS))
            pool.dma_start(h[:], h_spill[:, :, :]).then_inc(h_back, 16)
            pool.wait_ge(h_back, 16)

        @block.scalar
        def _(act):
            act.dma_start(bias_in[:], b_in).then_inc(const_in, 16)
            act.dma_start(gain[:], gains).then_inc(const_in, 16)
            act.dma_start(sink[:], sinks.partition_broadcast(P)).then_inc(const_in, 16)
            act.dma_start(tab[0:N_BUCKETS, :], rel_bias).then_inc(tab_in, 16)
            act.dma_start(hot[:], onehot).then_inc(tab_in, 16)

            def split_high(u, parity, slot, free=None):
                act.wait_ge(raw_in[parity], 8 * (u - parity) + 16)
                if free:
                    act.wait_ge(*free)
                nc.scalar.activation(wh[slot][:], raw[parity][:], ACT.Copy).then_inc(w_high, 1)

            def squares(norm, hf):
                for k in range(KT):
                    n = 16 * norm + 8 * hf + k
                    if norm == 0:
                        if k == 0:
                            act.wait_ge(x_in[hf], 16)
                    else:
                        act.wait_ge(down_added, (0, DOWN_MERGE, DOWN_FFN2, DOWN_FFN2 + 16 * FFN_STEPS)[norm] - 16 + 8 * hf + k + 1)
                    if n >= 2:
                        act.wait_ge(sq_sum, n - 1)
                    if k == 0 and hf and norm < 3:
                        act.wait_ge(x_low, 16 * norm + 8)
                    nc.scalar.activation(tmp[k % 2][:], h[:, k, hf * HALF:(hf + 1) * HALF], ACT.Square).then_inc(sq_done, 1)

            def root_of(norm, hf):
                act.wait_ge(made, 1)
                act.wait_ge(ssq, 2 * norm + hf + 1)
                if hf and norm == 3:
                    act.wait_ge(x_scaled, 16 * norm + 8)
                nc.scalar.activation(tmp[3][:], bank[NORM_BANK[hf]][:], ACT.Sqrt, scale=1.0 / D_MODEL,
                                     bias=eps[:, 0:1]).then_inc(root, 1)

            def norm_high(norm, hf):
                for k in range(KT):
                    act.wait_ge(x_scaled, 16 * norm + 8 * hf + k + 1)
                    nc.scalar.activation(xh[:, k, hf * HALF:(hf + 1) * HALF], tmp[k % 2][:], ACT.Copy).then_inc(x_high, 1)

            def norm(n, hf):
                squares(n, hf)
                root_of(n, hf)
                if n < 3:
                    norm_high(n, hf)

            def ffn_step(i, f, last=False):
                step = i + FFN_STEPS * f
                unit = FFN_UNITS * i + (FFN2_0 if f else 0)
                later = isinstance(i, int) and i == 0 and not f
                for t in range(4):
                    tile, hf = t % 2, t // 2
                    act.wait_ge(gu_done, 4 * step + t + 1)
                    if not (later and t < 2):
                        act.wait_ge(prod_done, 4 * step + t - 1)
                    nc.scalar.activation(tmp[t % 2][:], bank[2 * (t % 2)][:], ACT.Silu).then_inc(silu_done, 1)
                    if t < 2:
                        before = None if later else (down_done, 16 * step + (DOWN_FFN2 - 16 * FFN_STEPS if f else 0))
                        split_high(unit + 4 + t, t % 2, 4 + t, before)
                    act.wait_ge(prod_done, 4 * step + t + 1)
                    nc.scalar.activation(gh[:, tile, hf * HALF:(hf + 1) * HALF], tmp[2 + t % 2][:], ACT.Copy).then_inc(g_high, 1)
                if not (last and f):
                    for j in range(4):
                        split_high(unit + FFN_UNITS + j, j % 2, j, (gu_done, 4 * step + 3 + j // 2))

            for hf in range(2):
                norm(0, hf)
                if hf == 0:
                    for j in range(2):
                        split_high(j, j % 2, j)
                else:
                    for j in range(2, 4):
                        split_high(j, j % 2, j)
            act.wait_ge(x_low, 16)
            act.wait_ge(rows_out, 64)
            ffn_step(0, 0)
            with act.Fori(1, FFN_STEPS - 1) as i:
                ffn_step(i, 0)
            ffn_step(FFN_STEPS - 1, 0, last=True)
            for hf in range(2):
                norm(1, hf)

            act.wait_ge(bias_scaled, 1)
            tiles = proj_tiles()
            for e in PLAN:
                if e[0] == "ssq":
                    continue
                if e[0] == "job":
                    n, hf = JOBS[e[1]]
                    role, u = tiles[n]
                    _, _, g = unit_of(u)
                    last_qk = {"q": 8 * (u - 1), "k": 8 * (u - 1)}.get(role)
                    act.wait_ge(job_done, e[1] + 1)
                    if e[1] == 0:
                        act.wait_ge(spilled, 16 * 16)
                    if hf == 0 and u >= 2 and role != "v":
                        act.wait_ge(qk_done, last_qk)
                    if hf == 0 and role == "v" and u:
                        act.wait_ge(m_done, M_INDEX[("m", "v", u - 1, 1)] + 1)
                    dst = {"q": qs[u % 2], "k": ks[u % 2], "v": vt}[role]
                    src = bank[e[1] % 2][:] if g == 0 else bank[e[1] % 2][:].rearrange("p (q r) -> p q r", r=DILATIONS[g])
                    nc.scalar.activation(fold(dst, g, hf), src, ACT.Identity, scale=HD ** -0.5 if role == "q" else 1.0,
                                         bias=(bias_q if role == "q" else bias_in)[:, n:n + 1]).then_inc(job_out, 1)
                    if hf:
                        split_high(PROJ_0 + n + RING, n % 2, n % RING, (job_done, e[1] + 1))
                elif e[0] == "qk":
                    c = e[1]
                    u, a, j = c // 4, c // 2 % 2, c % 2
                    act.wait_ge(negm_done, c + 1)
                    for i in range(4):
                        lo = 0 if has_previous(u, 4 * j + i) else P
                        last = nc.scalar.activation(sp[c % 2][:, i, lo:], sp[c % 2][:, i, lo:], ACT.Exp,
                                                    bias=negm[:, 4 * c + i:4 * c + i + 1],
                                                    accum_out=den[:, 4 * c + i:4 * c + i + 1])
                    if u >= A_UNITS:
                        head = u - A_UNITS + B_UNITS * a
                        s = 4 * (c - 4 * A_UNITS)
                        last = nc.scalar.activation(sexp[:, s:s + 4], negm[:, 4 * c:4 * c + 4], ACT.Exp, bias=sink[:, head:head + 1])
                    last.then_inc(exp_done, 1)
                elif e[1] == "o" and e[2] >= A_UNITS:
                    i, hf = e[2] - A_UNITS, e[3]
                    act.wait_ge(m_done, M_INDEX[e] + 1)
                    if i < 2:
                        act.wait_ge(y_low, 4)
                    nc.scalar.activation(ybh[i][:, hf * HALF:(hf + 1) * HALF], bank[7][:], ACT.Copy).then_inc(yb_high, 1)
                elif e[1] == "stat":
                    pair = e[2]
                    u = 3 * pair + 2
                    act.wait_ge(pv_out, 4 * u + 4)
                    if pair:
                        act.wait_ge(m_done, M_INDEX[("m", "stat", 0)] + 1)
                    nc.scalar.activation(lse[:].rearrange("p g c -> p (g c)"), den[:, 48 * pair:48 * pair + 48], ACT.Ln).then_inc(ln_done, 1)
                elif e[1] == "lse" and e[4] == 2:
                    pair, hf = e[2], e[3]
                    act.wait_ge(mix_step, MIX_STEPS * (2 * pair + hf) + 5)
                    for g in range(3):
                        nc.scalar.activation(mix[pair][g][:], mix[pair][g][:], ACT.Exp).then_inc(mix_exp, 1)
                    act.wait_ge(mix_step, MIX_STEPS * (2 * pair + hf + 1))
                    nc.scalar.activation(yah[pair][:, hf * HALF:(hf + 1) * HALF], mix[pair][3][:], ACT.Copy).then_inc(ya_high, 1)

            def merge_step(i, last=False):
                unit = MERGE_0 + MERGE_UNITS * i
                nc.scalar.activation(gate_bias[:], bias_in[:, bass.ds(PROJ + 4 * i, 4)], ACT.Copy).then_inc(gate_bias_set, 1)
                act.wait_ge(gate_bias_set, i + 1)
                for t in range(4):
                    tile, hf = t // 2, t % 2
                    job = 4 * i + t
                    for gate in range(2):
                        act.wait_ge(part_done, 4 * job + 2 * gate + 1)
                        if not (isinstance(job, int) and job == 0):
                            act.wait_ge(mul_done, 3 * job)
                        nc.scalar.activation(tmp[gate][:], bank[2 * gate][:], ACT.Sigmoid,
                                             bias=gate_bias[:, 2 * tile + gate:2 * tile + gate + 1]).then_inc(sig_done, 1)
                        if hf:
                            j = 3 * tile + gate + RING
                            split_high(unit + j, j % 2, j % RING, (part_done, 4 * job + 2 * gate + 1))
                    act.wait_ge(mul_done, 3 * job + 3)
                    nc.scalar.activation(gh[:, tile, hf * HALF:(hf + 1) * HALF], tmp[2][:], ACT.Copy).then_inc(m_high, 1)
                    if hf:
                        j = 3 * tile + 2 + RING
                        split_high(unit + j, j % 2, j % RING, (part_done, 4 * job + 4))
                if last:
                    norm(2, 0)
                for j in range(2):
                    split_high(unit + 10 + j, j % 2, 2 + j, (down_done, DOWN_MERGE + 16 * i + 16))

            act.wait_ge(m_out, len(M_EVENTS))
            with act.Fori(0, MERGE_STEPS - 1) as i:
                merge_step(i)
            merge_step(MERGE_STEPS - 1, last=True)
            norm(2, 1)
            act.wait_ge(x_low, 48)
            with act.Fori(0, FFN_STEPS - 1) as i:
                ffn_step(i, 1)
            ffn_step(FFN_STEPS - 1, 1, last=True)
            for hf in range(2):
                norm(3, hf)

        @block.vector
        def _(dve):
            def split_low(u, parity, slot):
                dve.wait_ge(w_high, u + 1)
                nc.vector.tensor_tensor(wl[slot][:], raw[parity][:], wh[slot][:], ALU.subtract).then_inc(w_low, 1)

            def norm(norm, hf):
                cols = slice(hf * HALF, (hf + 1) * HALF)
                base = 16 * norm + 8 * hf
                for k in range(KT):
                    n = base + k
                    dve.wait_ge(sq_done, n + 1)
                    if k == 0:
                        nc.vector.tensor_copy(tmp[2][:], tmp[0][:]).then_inc(sq_sum, 1)
                    else:
                        dve.wait_ge(sq_sum, n)
                        nc.vector.tensor_tensor(tmp[2][:], tmp[2][:], tmp[k % 2][:], ALU.add).then_inc(sq_sum, 1)
                dve.wait_ge(root, 2 * norm + hf + 1)
                nc.vector.reciprocal(tmp[3][:], tmp[3][:]).then_inc(rstd_done, 1)
                dve.wait_ge(rstd_done, 2 * norm + hf + 1)
                if norm == 0 and hf == 0:
                    dve.wait_ge(const_in, 48)

                def low(k):
                    dve.wait_ge(x_high, base + k + 1)
                    nc.vector.tensor_tensor(xl[:, k, cols], tmp[k % 2][:], xh[:, k, cols], ALU.subtract).then_inc(x_low, 1)

                for k in range(KT):
                    if k >= 2 and norm < 3:
                        low(k - 2)
                        dve.wait_ge(x_low, base + k - 1)
                    nc.vector.scalar_tensor_tensor(out=tmp[k % 2][:] if norm < 3 else h[:, k, cols], in0=h[:, k, cols],
                                                   scalar=gain[:, norm, k:k + 1], in1=tmp[3][:], op0=ALU.mult,
                                                   op1=ALU.mult).then_inc(x_scaled, 1)
                if norm < 3:
                    low(KT - 2)
                    low(KT - 1)

            def ffn_step(i, f, last=False):
                step = i + FFN_STEPS * f
                unit = FFN_UNITS * i + (FFN2_0 if f else 0)
                for t in range(4):
                    tile, hf = t % 2, t // 2
                    dve.wait_ge(silu_done, 4 * step + t + 1)
                    if not (isinstance(i, int) and i == 0 and not f and t < 2):
                        dve.wait_ge(g_low, 4 * step + t - 1)
                    nc.vector.tensor_tensor(tmp[2 + t % 2][:], tmp[t % 2][:], bank[2 * (t % 2) + 1][:], ALU.mult).then_inc(prod_done, 1)
                    if t < 2:
                        split_low(unit + 4 + t, t % 2, 4 + t)
                    dve.wait_ge(g_high, 4 * step + t + 1)
                    cols = slice(hf * HALF, (hf + 1) * HALF)
                    nc.vector.tensor_tensor(gl[:, tile, cols], tmp[2 + t % 2][:], gh[:, tile, cols], ALU.subtract).then_inc(g_low, 1)
                first = 16 * step + (DOWN_FFN2 - 16 * FFN_STEPS if f else 0)
                for d in range(16):
                    hf, k = d // 8, d % 8
                    cols = slice(hf * HALF, (hf + 1) * HALF)
                    dve.wait_ge(down_done, first + d + 1)
                    nc.vector.scalar_tensor_tensor(out=h[:, k, cols], in0=bank[4 + d % 4][:], scalar=0.5, in1=h[:, k, cols],
                                                   op0=ALU.mult, op1=ALU.add).then_inc(down_added, 1)
                    if d % 4 == 1 and not (last and f):
                        split_low(unit + FFN_UNITS + d // 4, d // 4 % 2, d // 4)
                    if last and d == 7:
                        norm(1 + 2 * f, 0)

            for v, n in enumerate((4, 4, 4, 8)):
                dve.wait_ge(vec_done, v + 1)
                nc.vector.tensor_copy(rows[0:n, v, :], bank[v][0:n, 0:VEC]).then_inc(vec_out, 1)
            for hf in range(2):
                norm(0, hf)
                for j in range(2):
                    split_low(2 * hf + j, j, 2 * hf + j)
            ffn_step(0, 0)
            with dve.Fori(1, FFN_STEPS - 1) as i:
                ffn_step(i, 0)
            ffn_step(FFN_STEPS - 1, 0, last=True)
            norm(1, 1)
            nc.vector.tensor_scalar(bias_q[:], bias_in[:], HD ** -0.5, None, ALU.mult).then_inc(bias_scaled, 1)

            def combine(pair, hf):
                w, top, total = mix[pair][0:3], mix[pair][3], mix[pair][3]
                step = [MIX_STEPS * (2 * pair + hf)]
                cols = slice(hf * HALF, (hf + 1) * HALF)
                outs = [og[g][:, cols] for g in range(3)]

                def after(ins):
                    ins.then_inc(mix_step, 1)
                    step[0] += 1
                    dve.wait_ge(mix_step, step[0])

                if pair or hf:
                    dve.wait_ge(y_low, 2 * pair + hf)
                after(nc.vector.tensor_tensor(top[:], w[0][:], w[1][:], ALU.max))
                after(nc.vector.tensor_tensor(top[:], top[:], w[2][:], ALU.max))
                for g in range(3):
                    nc.vector.tensor_tensor(w[g][:], w[g][:], top[:], ALU.subtract).then_inc(mix_step, 1)
                step[0] += 3
                dve.wait_ge(mix_step, step[0])
                dve.wait_ge(mix_exp, 3 * (2 * pair + hf) + 3)
                after(nc.vector.tensor_tensor(total[:], w[0][:], w[1][:], ALU.add))
                after(nc.vector.tensor_tensor(total[:], total[:], w[2][:], ALU.add))
                after(nc.vector.reciprocal(total[:], total[:]))
                for g in range(3):
                    after(nc.vector.tensor_tensor(outs[g], outs[g], w[g][:], ALU.mult))
                after(nc.vector.tensor_tensor(outs[0], outs[0], outs[1], ALU.add))
                after(nc.vector.tensor_tensor(outs[0], outs[0], outs[2], ALU.add))
                after(nc.vector.tensor_tensor(top[:], outs[0], total[:], ALU.mult))
                assert step[0] == MIX_STEPS * (2 * pair + hf + 1)
                dve.wait_ge(ya_high, 2 * pair + hf + 1)
                nc.vector.tensor_tensor(yal[pair][:, cols], top[:], yah[pair][:, cols], ALU.subtract).then_inc(y_low, 1)

            for e in PLAN:
                if e[0] == "ssq":
                    continue
                if e[0] == "job":
                    n, hf = JOBS[e[1]]
                    if hf:
                        split_low(PROJ_0 + n + RING, n % 2, n % RING)
                elif e[0] == "qk":
                    c = e[1]
                    u, a, j = c // 4, c // 2 % 2, c % 2
                    kind, pair, g = unit_of(u)
                    for i in range(4):
                        lo = 0 if has_previous(u, 4 * j + i) else P
                        if i % 2 == 0:
                            dve.wait_ge(qk_done, 2 * c + i // 2 + 1)
                        head = pair + B_UNITS * a if kind == "B" else A_SLOTS * g + 2 * pair + a
                        bias = bias_B[:, head, lo:] if kind == "B" else bias_A[:, head, lo:] if g < 2 else bias_2[:, head - 2 * A_SLOTS, :]
                        nc.vector.tensor_tensor_reduce(out=sp[c % 2][:, i, lo:], in0=bank[2 + i // 2][:, i % 2 * 2 * P + lo:(i % 2 + 1) * 2 * P],
                                                       in1=bias, scale=1.0, scalar=3 * NEG, op0=ALU.add, op1=ALU.max,
                                                       accum_out=rmax[:, c % 2, i:i + 1]).then_inc(max_done, 1)
                    dve.wait_ge(max_done, 4 * c + 4)
                    floor = sink[:, head:head + 1] if kind == "B" else 3 * NEG
                    nc.vector.tensor_scalar(negm[:, 4 * c:4 * c + 4], rmax[:, c % 2, :], floor, -1.0, ALU.max, ALU.mult).then_inc(negm_done, 1)
                elif e[0] == "t":
                    c = e[1]
                    _, _, g = unit_of(c // 4)
                    for b in range(2):
                        dve.wait_ge(t_done, 2 * c + b + 1)
                        src = bank[4 + b][:].rearrange("p (i k) -> p i k", i=2)
                        dst = pt[c % 2][:, 2 * b:2 * b + 2, :]
                        if g == 2:
                            src, dst = src[:, :, P:], dst[:, :, P:]
                        elif not has_previous(c // 4, 4 * (c % 2) + 2 * b):
                            src = bank[4 + b][:, P:]
                            dst = dst.rearrange("p i k -> p (i k)")[:, P:]
                        nc.vector.tensor_copy(dst, src).then_inc(t_out, 1)
                elif e[0] == "pv":
                    c = e[1]
                    u, a, j = c // 4, c // 2 % 2, c % 2
                    total = den[:, 4 * c:4 * c + 4]
                    dve.wait_ge(pv_done, c + 1)
                    if u >= A_UNITS:
                        s = 4 * (c - 4 * A_UNITS)
                        nc.vector.tensor_tensor(total, total, sexp[:, s:s + 4], ALU.add).then_inc(den_done, 1)
                        dve.wait_ge(den_done, c + c - 4 * A_UNITS + 1)
                    nc.vector.reciprocal(rden[:, c % 2, :], total).then_inc(den_done, 1)
                    dve.wait_ge(den_done, c + 1 + max(0, c - 4 * A_UNITS + 1))
                    nc.vector.tensor_tensor(ob[:, 4 * j:4 * j + 4, a * HD:(a + 1) * HD],
                                            bank[6][:, 0:4 * HD].rearrange("p (i d) -> p i d", i=4),
                                            rden[:, c % 2, :].unsqueeze(2).to_broadcast([P, 4, HD]), ALU.mult).then_inc(pv_out, 1)
                else:
                    m = M_INDEX[e]
                    if e[1] == "stat":
                        pair = e[2]
                        dve.wait_ge(ln_done, pair + 1)
                        flat = lse[:].rearrange("p g c -> p (g c)")
                        nc.vector.tensor_tensor(flat, flat, negm[:, 48 * pair:48 * pair + 48], ALU.subtract).then_inc(lse_made, 1)
                    dve.wait_ge(m_done, m + 1)
                    if e[1] == "bias":
                        n = e[2]
                        src = bank[7][:].rearrange("p (h k) -> p h k", h=2)
                        if n < 4:
                            nc.vector.tensor_copy(bias_A[:, 2 * n:2 * n + 2, :], src).then_inc(m_out, 1)
                        elif n < 6:
                            nc.vector.tensor_copy(bias_2[:, 2 * n - 8:2 * n - 6, :], src[:, :, P:]).then_inc(m_out, 1)
                            if n == 5:
                                dve.wait_ge(m_out, m + 1)
                                nc.vector.memset(bias_2[HD:, :, 0:HD], NEG).then_inc(mask_set, 1)
                                dve.wait_ge(mask_set, 1)
                        else:
                            nc.vector.tensor_copy(bias_B[:, 2 * n - 12:2 * n - 10, :], src).then_inc(m_out, 1)
                    elif e[1] == "v":
                        u, hf = e[2], e[3]
                        nc.vector.tensor_copy(vs[u % 2][:, 4 * hf:4 * hf + 4, :], bank[7][:].rearrange("p (i d) -> p i d", i=4)).then_inc(m_out, 1)
                    elif e[1] == "o":
                        u, hf = e[2], e[3]
                        kind, i, g = unit_of(u)
                        if kind == "A":
                            dst = unfold(og[g], g, hf)
                            src = bank[7][:]
                            if g == 1:
                                src = src.rearrange("p (r b q) -> p r b q", r=2, b=2)
                            elif g == 2:
                                src = src.rearrange("p (r j) -> p r j", r=8)
                            nc.vector.tensor_copy(dst, src).then_inc(m_out, 1)
                        else:
                            cols = slice(hf * HALF, (hf + 1) * HALF)
                            dve.wait_ge(yb_high, 2 * i + hf + 1)
                            nc.vector.tensor_tensor(ybl[i][:, cols], bank[7][:], ybh[i][:, cols], ALU.subtract).then_inc(m_out, 1)
                    elif e[1] == "stat":
                        nc.vector.tensor_copy(lseT[:].rearrange("k g q -> k (g q)"), bank[7][0:16, 0:3 * P]).then_inc(m_out, 1)
                    elif e[1] == "lse":
                        pair, hf, g = e[2:]
                        nc.vector.tensor_copy(mix[pair][g][:], bank[7][:]).then_inc(m_out, 1)
                        if g == 2:
                            dve.wait_ge(m_out, m + 1)
                            combine(pair, hf)

            def merge_step(i, last=False):
                unit = MERGE_0 + MERGE_UNITS * i
                for t in range(4):
                    tile, hf = t // 2, t % 2
                    job = 4 * i + t
                    cols = slice(hf * HALF, (hf + 1) * HALF)
                    for gate in range(2):
                        dve.wait_ge(sig_done, 2 * job + gate + 1)
                        dve.wait_ge(part_done, 4 * job + 2 * gate + 2)
                        nc.vector.tensor_tensor(tmp[gate][:], tmp[gate][:], bank[2 * gate + 1][:], ALU.mult).then_inc(mul_done, 1)
                        if hf:
                            j = 3 * tile + gate + RING
                            split_low(unit + j, j % 2, j % RING)
                    dve.wait_ge(mul_done, 3 * job + 2)
                    if not (isinstance(job, int) and job == 0):
                        dve.wait_ge(m_low, job)
                    nc.vector.tensor_tensor(tmp[2][:], tmp[0][:], tmp[1][:], ALU.add).then_inc(mul_done, 1)
                    dve.wait_ge(m_high, job + 1)
                    nc.vector.tensor_tensor(gl[:, tile, cols], tmp[2][:], gh[:, tile, cols], ALU.subtract).then_inc(m_low, 1)
                    if hf:
                        j = 3 * tile + 2 + RING
                        split_low(unit + j, j % 2, j % RING)
                first = DOWN_MERGE + 16 * i
                for d in range(16):
                    hf, k = d // 8, d % 8
                    cols = slice(hf * HALF, (hf + 1) * HALF)
                    dve.wait_ge(down_done, first + d + 1)
                    nc.vector.tensor_tensor(h[:, k, cols], bank[4 + d % 4][:], h[:, k, cols], ALU.add).then_inc(down_added, 1)
                    if last and d == 7:
                        norm(2, 0)
                for j in range(2):
                    split_low(unit + 10 + j, j % 2, 2 + j)

            dve.wait_ge(h_back, 16)
            with dve.Fori(0, MERGE_STEPS - 1) as i:
                merge_step(i)
            merge_step(MERGE_STEPS - 1, last=True)
            norm(2, 1)
            with dve.Fori(0, FFN_STEPS - 1) as i:
                ffn_step(i, 1)
            ffn_step(FFN_STEPS - 1, 1, last=True)
            norm(3, 1)

        @block.tensor
        def _(pe):
            def product(out, slot, col, moving, first, last):
                hi, lo = moving
                cols = slice(col * P, (col + 1) * P)
                nc.tensor.matmul(out, wh[slot][:, cols], hi, start=first, stop=False)
                nc.tensor.matmul(out, wh[slot][:, cols], lo, start=False, stop=False)
                return nc.tensor.matmul(out, wl[slot][:, cols], hi, start=False, stop=last)

            def normed(k, hf):
                cols = slice(hf * HALF, (hf + 1) * HALF)
                return xh[:, k, cols], xl[:, k, cols]

            def gated(t, hf):
                cols = slice(hf * HALF, (hf + 1) * HALF)
                return gh[:, t, cols], gl[:, t, cols]

            def project(out, slot, hf, norm=None):
                for k in range(KT):
                    if norm is not None:
                        pe.wait_ge(x_low, 16 * norm + 8 * hf + k + 1)
                    last = product(out, slot, k, normed(k, hf), k == 0, k == KT - 1)
                return last

            def sum_squares(norm, hf):
                pe.wait_ge(made, 2)
                pe.wait_ge(sq_sum, 16 * norm + 8 * hf + 8)
                nc.tensor.matmul(bank[NORM_BANK[hf]][:], ones[:], tmp[2][:], start=True, stop=True).then_inc(ssq, 1)

            def ffn_step(i, f, last=False):
                step = i + FFN_STEPS * f
                unit = FFN_UNITS * i + (FFN2_0 if f else 0)
                first_step = isinstance(i, int) and i == 0
                for t in range(4):
                    tile, hf = t % 2, t // 2
                    if not (first_step and t < 2 and not f):
                        pe.wait_ge(prod_done, 4 * step + t - 1)
                    norm = 2 * f if first_step and tile == 0 else None
                    for part in range(2):
                        if hf == 0:
                            pe.wait_ge(w_low, unit + 2 * tile + part + 1)
                        done = project(bank[2 * (t % 2) + part][:], 2 * tile + part, hf, norm if part == 0 else None)
                    done.then_inc(gu_done, 1)
                    if first_step and t == 0:
                        sum_squares(2 * f, 1)
                first = 16 * step + (DOWN_FFN2 - 16 * FFN_STEPS if f else 0)
                pe.wait_ge(w_low, unit + 6)
                for d in range(16):
                    hf, k = d // 8, d % 8
                    if k == 0:
                        pe.wait_ge(g_low, 4 * step + 2 * hf + 2)
                    if not (first_step and not f and d < 4):
                        pe.wait_ge(down_added, first + d - 3)
                    for t in range(2):
                        done = product(bank[4 + d % 4][:], 4 + t, k, gated(t, hf), t == 0, t == 1)
                    done.then_inc(down_done, 1)
                    if last and d == 11:
                        sum_squares(1 + 2 * f, 0)

            pe.wait_ge(made, 5)
            pe.wait_ge(tab_in, 32)
            for v, (first, n) in enumerate(((0, 4), (4, 4), (8, 4), (12, 8))):
                nc.tensor.matmul(bank[v][0:n, 0:VEC], tab[:, first:first + n], hot[:, v, :], start=True, stop=True).then_inc(vec_done, 1)
            pe.wait_ge(vec_out, 4)
            sum_squares(0, 0)
            ffn_step(0, 0)
            with pe.Fori(1, FFN_STEPS - 1) as i:
                ffn_step(i, 0)
            ffn_step(FFN_STEPS - 1, 0, last=True)

            tiles = proj_tiles()
            for e in PLAN:
                if e[0] == "ssq":
                    sum_squares(1, 1)
                elif e[0] == "job":
                    n, hf = JOBS[e[1]]
                    if hf == 0:
                        pe.wait_ge(w_low, PROJ_0 + n + 1)
                    if e[1] >= 2:
                        pe.wait_ge(job_out, e[1] - 1)
                    project(bank[e[1] % 2][:], n % RING, hf, 1 if n == 0 else None).then_inc(job_done, 1)
                elif e[0] == "qk":
                    c = e[1]
                    u, a, j = c // 4, c // 2 % 2, c % 2
                    q_tile, k_tile = tiles.index(("q", u)), tiles.index(("k", min(u, A_UNITS)))
                    q, k = qs[u % 2], ks[min(u, A_UNITS) % 2]
                    part = slice(a * HD, (a + 1) * HD)
                    pe.wait_ge(job_out, JOB_INDEX[(max(q_tile, k_tile), 1)] + 1)
                    for i in range(4):
                        tile = 4 * j + i
                        lo = 0 if has_previous(u, tile) else P
                        if c and i % 2 == 0:
                            pe.wait_ge(max_done, 4 * (c - 1) + 2 * (i // 2) + 2)
                        last = nc.tensor.matmul(bank[2 + i // 2][:, i % 2 * 2 * P + lo:(i % 2 + 1) * 2 * P],
                                                q[part, tile * P:(tile + 1) * P],
                                                k[part, (tile - 1) * P + lo:(tile + 1) * P], start=True, stop=True)
                        if i % 2:
                            last.then_inc(qk_done, 1)
                elif e[0] == "t":
                    c = e[1]
                    u, j = c // 4, c % 2
                    pe.wait_ge(exp_done, c + 1)
                    for i in range(4):
                        if c and i % 2 == 0:
                            pe.wait_ge(t_out, 2 * (c - 1) + i // 2 + 1)
                        for b in range(0 if has_previous(u, 4 * j + i) else 1, 2):
                            last = nc.tensor.transpose(bank[4 + i // 2][:, (i % 2 * 2 + b) * P:(i % 2 * 2 + b + 1) * P],
                                                       sp[c % 2][:, i, b * P:(b + 1) * P], ident[:])
                        if i % 2:
                            last.then_inc(t_done, 1)
                elif e[0] == "pv":
                    c = e[1]
                    u, a, j = c // 4, c // 2 % 2, c % 2
                    vu = min(u, A_UNITS)
                    pe.wait_ge(m_out, M_INDEX[("m", "v", vu, 1)] + 1)
                    pe.wait_ge(t_out, 2 * c + 2)
                    if c:
                        pe.wait_ge(pv_out, c)
                    for i in range(4):
                        tile = 4 * j + i
                        start = 0 if has_previous(u, tile) else 1
                        for b in range(start, 2):
                            last = nc.tensor.matmul(bank[6][:, i * HD:(i + 1) * HD], pt[c % 2][:, i, b * P:(b + 1) * P],
                                                    vs[vu % 2][:, tile - 1 + b, a * HD:(a + 1) * HD], start=b == start, stop=b == 1)
                    last.then_inc(pv_done, 1)
                else:
                    m = M_INDEX[e]
                    if m:
                        pe.wait_ge(m_out, m)
                    if e[1] == "bias":
                        if e[2] == 0:
                            pe.wait_ge(skew_in, 16)
                            pe.wait_ge(made, 7)
                        last = nc.tensor.matmul(bank[7][:], flip[:], skew[:, 2 * e[2]:2 * e[2] + 2, :].rearrange("p h k -> p (h k)"),
                                                start=True, stop=True)
                    elif e[1] == "v":
                        u, hf = e[2], e[3]
                        pe.wait_ge(job_out, JOB_INDEX[(tiles.index(("v", u)), 1)] + 1)
                        for i in range(4):
                            last = nc.tensor.transpose(bank[7][:, i * P:(i + 1) * P], vt[:, (4 * hf + i) * P:(4 * hf + i + 1) * P], ident[:])
                    elif e[1] == "o":
                        u, hf = e[2], e[3]
                        pe.wait_ge(pv_out, 4 * u + 4)
                        for i in range(4):
                            last = nc.tensor.transpose(bank[7][:, i * P:(i + 1) * P], ob[:, 4 * hf + i, :], ident[:])
                    elif e[1] == "stat":
                        pe.wait_ge(lse_made, e[2] + 1)
                        for g in range(3):
                            last = nc.tensor.transpose(bank[7][0:16, g * P:(g + 1) * P], lse[:, g, :], ident[:])
                    else:
                        _, _, pair, hf, g = e
                        pe.wait_ge(sel_made, 2)
                        for i in range(4 if g < 2 else 8):
                            tile = 4 * hf + i if g == 0 else 2 * i + hf if g == 1 else i
                            src = lseT[:, g, :]
                            if g == 0:
                                out = bank[7][:, i * P:(i + 1) * P]
                            elif g == 1:
                                out = bank[7][:].rearrange("p (q r) -> p r q", r=4)[:, i, :]
                            else:
                                src = src.rearrange("k (s j) -> k s j", s=2)[:, :, 32 * hf:32 * hf + 32]
                                out = bank[7][:].rearrange("p (j r) -> p r j", r=16)[:, 2 * i:2 * i + 2, :]
                            last = nc.tensor.matmul(out, sel[:, tile, :], src, start=True, stop=True)
                    last.then_inc(m_done, 1)

            def merge_step(i, last=False):
                unit = MERGE_0 + MERGE_UNITS * i
                first_step = isinstance(i, int) and i == 0
                for t in range(4):
                    tile, hf = t // 2, t % 2
                    job = 4 * i + t
                    cols = slice(hf * HALF, (hf + 1) * HALF)
                    for part in range(4):
                        gate = part // 2
                        if hf == 0 and part != 3:
                            pe.wait_ge(w_low, unit + 3 * tile + (0, 2, 1)[part] + 1 if part != 1 else unit + 3 * tile + 3)
                        if not (first_step and t == 0):
                            if part % 2:
                                pe.wait_ge(mul_done, 3 * job - 2 + gate)
                            else:
                                pe.wait_ge(sig_done, 2 * job - 1 + gate)
                        slot = (3 * tile + gate) % RING
                        if part % 2 == 0:
                            done = project(bank[part][:], slot, hf)
                        else:
                            slot = (3 * tile + 2) % RING
                            ys = [(yah[p], yal[p]) for p in range(2)] if gate == 0 else [(ybh[p], ybl[p]) for p in range(B_UNITS)]
                            for p, (hi, lo) in enumerate(ys):
                                done = product(bank[part][:], slot, 2 * gate + p, (hi[:, cols], lo[:, cols]), p == 0, p == len(ys) - 1)
                        done.then_inc(part_done, 1)
                pe.wait_ge(w_low, unit + 8)
                first = DOWN_MERGE + 16 * i
                for d in range(16):
                    hf, k = d // 8, d % 8
                    if k == 0:
                        pe.wait_ge(m_low, 4 * i + 3 + hf)
                    pe.wait_ge(down_added, first + d - 3)
                    for t in range(2):
                        done = product(bank[4 + d % 4][:], 2 + t, k, gated(t, hf), t == 0, t == 1)
                    done.then_inc(down_done, 1)
                    if last and d == 11:
                        sum_squares(2, 0)

            pe.wait_ge(job_out, 2 * PROJ)
            pe.wait_ge(max_done, 4 * CHUNKS)
            pe.wait_ge(t_out, 2 * CHUNKS)
            pe.wait_ge(pv_out, CHUNKS)
            pe.wait_ge(m_out, len(M_EVENTS))
            merge_step(0)
            with pe.Fori(1, MERGE_STEPS - 1) as i:
                merge_step(i)
            merge_step(MERGE_STEPS - 1, last=True)
            ffn_step(0, 1)
            with pe.Fori(1, FFN_STEPS - 1) as i:
                ffn_step(i, 1)
            ffn_step(FFN_STEPS - 1, 1, last=True)
            sum_squares(3, 1)


NORM_BANK = (0, 4)
MIX_STEPS = 14


def kernel(x, ffn1_norm, ffn1_w_gate, ffn1_w_up, ffn1_w_down, mix_norm, w_in, b_in, w_branch_a, w_branch_b, w_out,
           sinks, rel_bias, ffn2_norm, ffn2_w_gate, ffn2_w_up, ffn2_w_down, final_norm):
    import concourse.bacc as bacc
    from concourse.bass_utils import run_bass_kernel_spmd

    stream = np.zeros((N_UNITS, P, UNIT), np.float32)
    at = iter(range(N_UNITS))

    def columns(w, cols):
        stream[next(at)] = w[:, cols].reshape(KT, P, P).transpose(1, 0, 2).reshape(P, UNIT)

    def ffn(gate, up, down):
        for i in range(FFN_STEPS):
            for t in (2 * i, 2 * i + 1):
                columns(gate, np.arange(t * P, (t + 1) * P))
                columns(up, np.arange(t * P, (t + 1) * P))
            for t in (2 * i, 2 * i + 1):
                stream[next(at)] = down[t * P:(t + 1) * P, :]

    w = np.asarray(w_in[0])
    b = np.asarray(b_in[0])
    ffn(np.asarray(ffn1_w_gate[0]), np.asarray(ffn1_w_up[0]), np.asarray(ffn1_w_down[0]))
    order = [head_columns(role, u) for role, u in proj_tiles()]
    for cols in order:
        columns(w, cols)
    gates = D_IN - 2 * D_MODEL
    wa, wo = np.asarray(w_branch_a[0]), np.asarray(w_out[0])
    wb = np.asarray(w_branch_b[0]).reshape(2, B_UNITS, HD, D_MODEL).transpose(1, 0, 2, 3).reshape(B_HEADS * HD, D_MODEL)
    for i in range(MERGE_STEPS):
        for t in (2 * i, 2 * i + 1):
            pair = [np.arange(gates + g * D_MODEL + t * P, gates + g * D_MODEL + (t + 1) * P) for g in range(2)]
            order += pair
            for cols in pair:
                columns(w, cols)
            both = np.concatenate([wa, wb])[:, t * P:(t + 1) * P].reshape(6, P, P).transpose(1, 0, 2).reshape(P, 6 * P)
            stream[next(at), :, 0:6 * P] = both
        for t in (2 * i, 2 * i + 1):
            stream[next(at)] = wo[t * P:(t + 1) * P, :]
    ffn(np.asarray(ffn2_w_gate[0]), np.asarray(ffn2_w_up[0]), np.asarray(ffn2_w_down[0]))

    norms = [np.asarray(ffn1_norm[0]), np.asarray(mix_norm[0]), np.asarray(ffn2_norm[0]), np.asarray(final_norm)]
    arrays = {
        "xT": np.ascontiguousarray(np.asarray(x[0]).T),
        "stream": stream,
        "gains": np.ascontiguousarray(np.stack(norms).reshape(4, KT, P).transpose(2, 0, 1)),
        "b_in": np.ascontiguousarray(np.stack([b[c] for c in order]).T),
        "sinks": np.ascontiguousarray(np.asarray(sinks[0])),
        "rel_bias": np.ascontiguousarray(np.asarray(rel_bias)),
        "onehot": distance_onehot(),
    }
    nc = bacc.Bacc("TRN2", target_bir_lowering=False, num_devices=1)
    args = [nc.dram_tensor(n, a.shape, mybir.dt.from_np(a.dtype), kind="ExternalInput").ap() for n, a in arrays.items()]
    bias_rows = nc.dram_tensor("bias_rows", (HEADS, VEC), mybir.dt.float32, kind="Internal").ap()
    h_spill = nc.dram_tensor("h_spill", (P, KT, SEQ), mybir.dt.float32, kind="Internal").ap()
    outT = nc.dram_tensor("outT", (D_MODEL, SEQ), mybir.dt.float32, kind="ExternalOutput").ap()
    build(nc, *args, bias_rows, h_spill, outT)
    r = run_bass_kernel_spmd(nc, [arrays], core_ids=[0])
    return np.ascontiguousarray(r.results[0]["outT"].T)[None]
```

```python
import math
from contextlib import ExitStack

import numpy as np

import concourse.bass as bass
from concourse import mybir

P = 128
D_MODEL, SEQ, D_FF = 1024, 1024, 2816
HD = 64
EPS = 1e-6
DILATIONS = (1, 4, 16)
WINDOWS = (128, 512, 2048)
A_SLOTS = 4
A_HEADS, B_HEADS, B_KV = 12, 8, 2
B_WINDOW = 128
N_BUCKETS, MAX_DISTANCE = 32, 2048
HEADS = A_HEADS + B_HEADS
D_IN = 3 * A_HEADS * HD + B_HEADS * HD + 2 * B_KV * HD + 2 * D_MODEL

KT = D_MODEL // P
HALF = SEQ // 2
FT = D_FF // P
FFN_STEPS = FT // 2
UNIT = 1024
FFN_UNITS = 6
A_UNITS = 6
B_UNITS = 4
HEAD_UNITS = A_UNITS + B_UNITS
PROJ = 3 * A_UNITS + 2 + B_UNITS
MERGE_STEPS = KT // 2
MERGE_UNITS = 8
PROJ_0 = FFN_UNITS * FFN_STEPS
MERGE_0 = PROJ_0 + PROJ
FFN2_0 = MERGE_0 + MERGE_UNITS * MERGE_STEPS
N_UNITS = FFN2_0 + FFN_UNITS * FFN_STEPS
RING = 4
CHUNKS = 4 * HEAD_UNITS
QT = SEQ // P
BIN_TILES = D_IN // P
NEG = -1e30
VEC = 384



def unit_of(u):
    return ("A", u // 3, u % 3) if u < A_UNITS else ("B", u - A_UNITS, 0)


def proj_tiles():
    out = []
    for u in range(A_UNITS + 1):
        out += [("q", u), ("k", u), ("v", u)]
    return out + [("q", u) for u in range(A_UNITS + 1, HEAD_UNITS)]


def head_columns(role, u):
    kind, a, g = unit_of(u)
    qa, qb = 0, 3 * A_HEADS * HD
    if kind == "A":
        at = {"q": 0, "k": 1, "v": 2}[role] * A_HEADS * HD + (A_SLOTS * g + 2 * a) * HD
        return np.arange(at, at + P)
    if role == "q":
        return np.concatenate([np.arange(qb + h * HD, qb + (h + 1) * HD) for h in (a, a + B_HEADS // 2)])
    at = qb + B_HEADS * HD + (0 if role == "k" else B_KV * HD)
    return np.arange(at, at + P)


def bucket(dist):
    max_exact = N_BUCKETS // 2
    n = np.maximum(dist, 0)
    nf = np.maximum(n, 1).astype(np.float32)
    large = max_exact + (np.log(nf / np.float32(max_exact)) / np.float32(math.log(MAX_DISTANCE / max_exact))
                         * np.float32(N_BUCKETS - max_exact)).astype(np.int32)
    return np.where(n < max_exact, n, np.minimum(large, N_BUCKETS - 1))


def distance_onehot():
    out = np.zeros((N_BUCKETS + 1, 4, VEC), np.float32)
    steps = [(d, w // d) for w, d in zip(WINDOWS, DILATIONS)] + [(1, B_WINDOW - 1)]
    for v, (d, most) in enumerate(steps):
        for j in range(VEC):
            dist = 2 * P - 1 - j
            row = int(bucket(np.array(dist * d))) if 0 <= dist <= most else N_BUCKETS
            out[row, v, j] = 1.0
    return out


JOBS = [(n, hf) for hf in range(2) for n in range(2)] + [(n, hf) for n in range(2, PROJ) for hf in range(2)]
JOB_INDEX = {job: j for j, job in enumerate(JOBS)}


def attention_plan():
    plan = []
    jobs = iter(range(2 * PROJ))

    def job(n=1):
        for _ in range(n):
            plan.append(("job", next(jobs)))

    job(2)
    plan.append(("ssq",))
    job(2)
    for i in range(HEADS // 2):
        plan.append(("m", "bias", i))
        if i in (3, 7):
            job()
    plan.append(("m", "v", 0, 0))
    for u in range(HEAD_UNITS + 1):
        for s in range(4):
            c = 4 * u + s
            if c < CHUNKS:
                plan.append(("qk", c))
            n_jobs = (1, 2, 1, 2)[s] if u < A_UNITS else (0, 1, 0, 1)[s] if u < HEAD_UNITS - 1 else 0
            if n_jobs:
                job()
            if s == 0 and u <= A_UNITS:
                plan.append(("m", "v", u, 1))
            done = {4: 0, 5: 1, 7: 2, 8: 3}.get(u)
            if s == 2 and done is not None:
                plan.append(("mix", "y", done))
            if s == 2 and u:
                plan.append(("m", "o", u - 1, 0))
            if s == 3 and u:
                plan.append(("m", "o", u - 1, 1))
            if s == 2 and u in (3, 6):
                plan.append(("m", "stat", u // 3 - 1))
            start = {3: 0, 4: 1, 6: 2, 7: 3}.get(u)
            if s == 3 and start is not None:
                plan += [("m", "lse", start // 2, start % 2, g) for g in range(3)]
            if 0 <= c - 1 < CHUNKS:
                plan.append(("t", c - 1))
            if 0 <= c - 2 < CHUNKS:
                plan.append(("pv", c - 2))
            if n_jobs == 2:
                job()
            if s == 3 and start is not None:
                plan.append(("mix", "exp", start))
            if s == 1 and done is not None:
                plan.append(("mix", "inv", done))
            if s == 3 and u < A_UNITS:
                plan.append(("m", "v", u + 1, 0))
    assert next(jobs, None) is None
    return plan


PLAN = attention_plan()
M_EVENTS = [e for e in PLAN if e[0] == "m"]
M_INDEX = {e: n for n, e in enumerate(M_EVENTS)}


def build(nc, xT, stream, gains, b_in, sinks, rel_bias, onehot, bias_rows, h_spill, outT):
    f32, f32r = mybir.dt.float32, mybir.dt.float32r
    ALU = mybir.AluOpType
    ACT = mybir.ActivationFunctionType

    BASE = 4224
    K = 1024
    names = iter(range(1000))

    def place(name, shape, offset, dtype=f32):
        return nc.alloc_sbuf_tensor_at(f"{name}_{next(names)}", shape, dtype, offset=BASE + offset)

    ident = place("ident", [P, P], 0)
    ones = place("ones", [P, P], 512)
    bias_in = place("bias_in", [P, BIN_TILES], 1024)
    bias_q = place("bias_q", [P, BIN_TILES], 1184)
    gain = place("gain", [P, 4, KT], 1344)
    sink = place("sink", [P, B_HEADS], 1472)
    eps = place("eps", [P, 1], 1504)
    gate_bias = place("gate_bias", [P, 4], 1536)
    R = 1568

    def at(k):
        return R + int(k * K)

    h = place("h", [P, KT, SEQ], at(0))
    xh = place("xh", [P, KT, SEQ], at(32), f32r)
    xl = place("xl", [P, KT, SEQ], at(64), f32r)
    wh = [place(f"wh{s}", [P, UNIT], at(96 + 8 * s), f32r) for s in range(FFN_UNITS)]
    wl = [place(f"wl{s}", [P, UNIT], at(100 + 8 * s), f32r) for s in range(FFN_UNITS)]
    raw = [place(f"raw{s}", [P, UNIT], at(144 + 4 * s)) for s in range(2)]
    gh = place("gh", [P, 2, SEQ], at(152), f32r)
    gl = place("gl", [P, 2, SEQ], at(160), f32r)
    tmp = [place(f"tmp{s}", [P, HALF], at(168 + 2 * s)) for s in range(4)]
    rows = place("rows", [B_HEADS, 4, VEC], at(176))
    skew = place("skew", [P, HEADS, 2 * P], at(176))
    flip = place("flip", [P, P], at(196))
    tab = place("tab", [N_BUCKETS + 1, HEADS], at(197))
    hot = place("hot", [N_BUCKETS + 1, 4, VEC], at(198))
    rstd = place("rstd", [P, SEQ], at(206))
    acc = [place(f"acc{s}", [P, HALF], at(210 + 2 * s)) for s in range(2)]
    sq = [place(f"sq{s}", [P, HALF], at(214 + 2 * s)) for s in range(2)]
    qs = [place("q0", [P, SEQ], at(0)), place("q1", [P, SEQ], at(4))]
    ks = [place("k0", [P, SEQ], at(8)), place("k1", [P, SEQ], at(190))]
    vs = [place("v0", [P, QT, P], at(12)), place("v1", [P, QT, P], at(194))]
    vt = place("vt", [P, SEQ], at(16))
    ob = place("ob", [P, QT, P], at(20))
    sp = [place(f"sp{s}", [P, 4, 2 * P], at(24 + 4 * s)) for s in range(2)]
    bias_B = place("bias_B", [P, B_HEADS, 2 * P], at(152))
    pt = [place(f"pt{s}", [P, 4, 2 * P], at(160 + 4 * s)) for s in range(2)]
    bias_2 = place("bias_2", [P, A_SLOTS, P], at(168))
    negm = place("negm", [P, 4 * CHUNKS], at(170))
    den = place("den", [P, 4 * CHUNKS], at(170) + 640)
    sexp = place("sexp", [P, 4 * 4 * B_UNITS], at(170) + 1280)
    lse = place("lse", [P, 3, 16], at(170) + 1536)
    rmax = place("rmax", [P, 2, 4], at(170) + 1728)
    rden = place("rden", [P, 2, 4], at(170) + 1760)
    lseT = place("lseT", [16, 3, P], at(170) + 2048)
    bias_A = place("bias_A", [P, 2 * A_SLOTS, 2 * P], at(198))
    Y = [174 + 4 * n for n in range(8)] + [128 + 4 * n for n in range(4)]
    yah = [place(f"yah{p}", [P, SEQ], at(Y[2 * p]), f32r) for p in range(2)]
    yal = [place(f"yal{p}", [P, SEQ], at(Y[2 * p + 1]), f32r) for p in range(2)]
    og = [place(f"og{g}", [P, SEQ], at((Y[8], Y[9], Y[10], 210)[g])) for g in range(4)]
    scaled = [place(f"scaled{s}", [P, HALF], at(214 + 2 * s)) for s in range(2)]
    sel = place("sel", [16, QT, P], at(Y[11]))
    YB = (6, 10, 8, 4)
    ybh = [place(f"ybh{i}", [P, SEQ], at(Y[YB[i]]), f32r) for i in range(B_UNITS)]
    ybl = [place(f"ybl{i}", [P, SEQ], at(Y[YB[i] + 1]), f32r) for i in range(B_UNITS)]
    mix = [[place(f"mix{p}{n}", [P, HALF], at(Y[(2, 4)[p]] + 2 * n)) for n in range(4)] for p in range(2)]

    ctx = ExitStack()
    with ctx:
        bank = [ctx.enter_context(nc.psum_tensor(f"bank{n}", [P, HALF], f32)) for n in range(8)]

        def sem(name):
            return ctx.enter_context(nc.semaphore(name))

        x_in = [sem(f"x_in{n}") for n in range(5)]
        const_in = sem("const_in")
        tab_in = sem("tab_in")
        raw_in = [sem("raw_in0"), sem("raw_in1")]
        rows_out = sem("rows_out")
        skew_in = sem("skew_in")
        spilled = sem("spilled")
        h_back = sem("h_back")
        stored = sem("stored")
        made = sem("made")
        bias_scaled = sem("bias_scaled")
        sel_made = sem("sel_made")
        vec_done = sem("vec_done")
        vec_out = sem("vec_out")
        w_high = sem("w_high")
        w_low = sem("w_low")
        sq_done = sem("sq_done")
        sq_sum = sem("sq_sum")
        ssq = sem("ssq")
        root = sem("root")
        rstd_done = sem("rstd_done")
        x_high = sem("x_high")
        x_low = sem("x_low")
        x_out = sem("x_out")
        gu_done = sem("gu_done")
        gu_out = sem("gu_out")
        silu_done = sem("silu_done")
        prod_done = sem("prod_done")
        g_high = sem("g_high")
        g_low = sem("g_low")
        down_done = sem("down_done")
        down_added = sem("down_added")
        job_done = sem("job_done")
        job_scaled = sem("job_scaled")
        job_out = sem("job_out")
        qk_done = sem("qk_done")
        max_done = sem("max_done")
        negm_done = sem("negm_done")
        exp_done = sem("exp_done")
        t_done = sem("t_done")
        t_out = [sem("t_out0"), sem("t_out1")]
        pv_done = sem("pv_done")
        den_done = sem("den_done")
        pv_out = sem("pv_out")
        m_done = sem("m_done")
        m_out = sem("m_out")
        mask_set = sem("mask_set")
        yb_high = sem("yb_high")
        ln_done = sem("ln_done")
        lse_made = sem("lse_made")
        mix_top = sem("mix_top")
        mix_diff = sem("mix_diff")
        mix_exp = sem("mix_exp")
        mix_sum = sem("mix_sum")
        mix_inv = sem("mix_inv")
        mix_part = sem("mix_part")
        mix_y = sem("mix_y")
        ya_high = sem("ya_high")
        y_low = sem("y_low")
        part_done = sem("part_done")
        gate_bias_set = sem("gate_bias_set")
        sig_done = sem("sig_done")
        mul_done = sem("mul_done")
        m_high = sem("m_high")
        m_low = sem("m_low")

        block = ctx.enter_context(nc.Block())

        def fold(buf, g, hf):
            if g == 0:
                return buf[:, hf * HALF:(hf + 1) * HALF]
            d = DILATIONS[g]
            n = HALF // d
            return buf[:, :].rearrange("p (r b q) -> p q r b", r=d, b=2)[:, 0:n, :, hf]

        def unfold(buf, g, hf):
            if g == 0:
                return buf[:, hf * HALF:(hf + 1) * HALF]
            if g == 1:
                return buf[:, :].rearrange("p (b q r) -> p r b q", b=2, r=4)[:, 2 * hf:2 * hf + 2]
            return buf[:, :].rearrange("p (j r) -> p r j", r=16)[:, 8 * hf:8 * hf + 8]

        def has_previous(u, tile):
            kind, _, g = unit_of(u)
            return tile > 0 if g == 0 else g == 1 and tile % 2 == 1

        def transposed(c, b):
            _, _, g = unit_of(c // 4)
            src = bank[4 + b][:].rearrange("p (i k) -> p i k", i=2)
            dst = pt[c % 2][:, 2 * b:2 * b + 2, :]
            if g == 2:
                return dst[:, :, P:], src[:, :, P:]
            if not has_previous(c // 4, 4 * (c % 2) + 2 * b):
                return dst.rearrange("p i k -> p (i k)")[:, P:], bank[4 + b][:, P:]
            return dst, src

        DOWN_MERGE = 16 * FFN_STEPS
        DOWN_FFN2 = DOWN_MERGE + 16 * MERGE_STEPS

        @block.sync
        def _(sp_):
            x_t = xT.rearrange("(k p) t -> p k t", p=P)
            sp_.dma_start(raw[0][:], stream[0]).then_inc(raw_in[0], 16)
            for n in range(4):
                sp_.dma_start(h[:, 2 * n:2 * n + 2, 0:HALF], x_t[:, 2 * n:2 * n + 2, 0:HALF]).then_inc(x_in[n], 16)
                if n == 1:
                    sp_.dma_start(raw[1][:], stream[1]).then_inc(raw_in[1], 16)
            sp_.dma_start(h[:, :, HALF:], x_t[:, :, HALF:]).then_inc(x_in[4], 16)
            with sp_.Fori(1, N_UNITS // 2) as n:
                for s in range(2):
                    sp_.wait_ge(w_low, 2 * n - 1 + s)
                    sp_.dma_start(raw[s][:], stream[2 * n + s]).then_inc(raw_in[s], 16)
            for hf in range(2):
                for k in range(KT):
                    cols = slice(hf * HALF, (hf + 1) * HALF)
                    sp_.wait_ge(x_out, 8 * hf + k + 1)
                    sp_.dma_start(outT[k * P:(k + 1) * P, cols], h[:, k, cols]).then_inc(stored, 16)
            sp_.wait_ge(stored, 16 * 16)

        @block.gpsimd
        def _(pool):
            nc.gpsimd.memset(eps[:], EPS).then_inc(made, 1)
            nc.gpsimd.memset(ones[:], 1.0).then_inc(made, 1)
            nc.gpsimd.memset(ident[:], 0.0).then_inc(made, 1)
            nc.gpsimd.memset(flip[:], 0.0).then_inc(made, 1)
            pool.wait_ge(made, 4)
            nc.gpsimd.memset(tab[N_BUCKETS:, :], NEG).then_inc(made, 1)
            pool.wait_ge(made, 5)
            nc.gpsimd.affine_select(out=ident[:], in_=ident[:], compare_op=ALU.not_equal, fill=1.0, base=0,
                                    pattern=[[-1, P]], channel_multiplier=1).then_inc(made, 1)
            nc.gpsimd.affine_select(out=flip[:], in_=flip[:], compare_op=ALU.not_equal, fill=1.0,
                                    base=1 - P, pattern=[[1, P]], channel_multiplier=1).then_inc(made, 1)

            def add_squares(norm, hf):
                base = (KT - 1) * (2 * norm + hf)
                for k in range(1, KT):
                    pool.wait_ge(sq_done, 16 * norm + 8 * hf + k + 1)
                    if k > 1:
                        pool.wait_ge(sq_sum, base + k - 1)
                    nc.gpsimd.tensor_tensor(acc[hf][:], (sq[0] if k == 1 else acc[hf])[:], sq[k % 2][:], ALU.add).then_inc(sq_sum, 1)

            add_squares(0, 0)
            add_squares(0, 1)
            pool.wait_ge(vec_out, 4)
            for v, (first, n) in enumerate(((0, 4), (4, 4), (8, 4), (12, 8))):
                pool.dma_start(bias_rows[first:first + n, :], rows[0:n, v, :]).then_inc(rows_out, 16)
            pool.wait_ge(rows_out, 64)
            pool.dma_start(skew[:], bass.AP(tensor=bias_rows.tensor, offset=bias_rows.offset,
                                            ap=[[1, P], [VEC, HEADS], [1, 2 * P]])).then_inc(skew_in, 16)
            add_squares(1, 0)
            add_squares(1, 1)
            pool.wait_ge(down_done, DOWN_MERGE)
            nc.gpsimd.memset(sel[:], 0.0).then_inc(sel_made, 1)
            pool.wait_ge(sel_made, 1)
            nc.gpsimd.affine_select(out=sel[:].rearrange("k t (s c) -> k t s c", s=2),
                                    in_=sel[:].rearrange("k t (s c) -> k t s c", s=2),
                                    compare_op=ALU.not_equal, fill=1.0, base=0,
                                    pattern=[[-1, QT], [-QT, 2], [0, HD]], channel_multiplier=1).then_inc(sel_made, 1)

            for n in range(4):
                pair, hf = n // 2, n % 2
                w, total = mix[pair][0:3], mix[pair][3]
                outs = [og[(3 * pair + g) % 4][:, hf * HALF:(hf + 1) * HALF] for g in range(3)]
                pool.wait_ge(mix_top, 2 * n + 2)
                for g in range(3):
                    nc.gpsimd.tensor_tensor(w[g][:], w[g][:], total[:], ALU.subtract).then_inc(mix_diff, 1)
                pool.wait_ge(mix_exp, 3 * n + 2)
                pool.wait_ge(mix_diff, 3 * n + 3)
                nc.gpsimd.tensor_tensor(total[:], w[0][:], w[1][:], ALU.add).then_inc(mix_sum, 1)
                pool.wait_ge(mix_exp, 3 * n + 3)
                pool.wait_ge(mix_sum, 2 * n + 1)
                nc.gpsimd.tensor_tensor(total[:], total[:], w[2][:], ALU.add).then_inc(mix_sum, 1)
                pool.wait_ge(m_out, M_INDEX[("m", "o", 3 * pair + 2, 1)] + 1)
                for g in range(3):
                    nc.gpsimd.tensor_tensor(outs[g], outs[g], w[g][:], ALU.mult).then_inc(mix_part, 1)
                pool.wait_ge(mix_part, 5 * n + 2)
                nc.gpsimd.tensor_tensor(outs[0], outs[0], outs[1], ALU.add).then_inc(mix_part, 1)
                pool.wait_ge(mix_part, 5 * n + 4)
                nc.gpsimd.tensor_tensor(outs[0], outs[0], outs[2], ALU.add).then_inc(mix_part, 1)
                pool.wait_ge(mix_part, 5 * n + 5)
                pool.wait_ge(mix_inv, n + 1)
                nc.gpsimd.tensor_tensor(total[:], outs[0], total[:], ALU.mult).then_inc(mix_y, 1)
            for norm in (2, 3):
                for hf in range(2):
                    add_squares(norm, hf)

        @block.scalar
        def _(act):
            act.dma_start(bias_in[:], b_in).then_inc(const_in, 16)
            act.dma_start(gain[:], gains).then_inc(const_in, 16)
            act.dma_start(sink[:], sinks.partition_broadcast(P)).then_inc(const_in, 16)
            act.dma_start(tab[0:N_BUCKETS, :], rel_bias).then_inc(tab_in, 16)
            act.dma_start(hot[:], onehot).then_inc(tab_in, 16)

            def split_high(u, parity, slot, free=None):
                act.wait_ge(raw_in[parity], 8 * (u - parity) + 16)
                if free:
                    act.wait_ge(*free)
                nc.scalar.activation(wh[slot][:], raw[parity][:], ACT.Copy).then_inc(w_high, 1)

            def prepare(norm, hf, k):
                cols = slice(hf * HALF, (hf + 1) * HALF)
                base = (KT - 1) * (2 * norm + hf)
                if norm == 0:
                    act.wait_ge(x_in[k // 2 if hf == 0 else 4], 16)
                else:
                    first = (0, DOWN_MERGE, DOWN_FFN2, DOWN_FFN2 + 16 * FFN_STEPS)[norm] - 16
                    act.wait_ge(down_added, first + 8 * hf + k + 1)
                if norm < 3:
                    if norm == 0 and hf == 0 and k == 0:
                        act.wait_ge(const_in, 48)
                    nc.scalar.activation(xh[:, k, cols], h[:, k, cols], ACT.Copy, scale=gain[:, norm, k:k + 1]).then_inc(x_high, 1)
                free = base - 1 + k if k < 2 else base + max(1, k - 2)
                if free > 0:
                    act.wait_ge(sq_sum, free)
                nc.scalar.activation(sq[k % 2][:], h[:, k, cols], ACT.Square).then_inc(sq_done, 1)
                if norm == 1:
                    act.dma_start(h_spill[:, k, cols], h[:, k, cols]).then_inc(spilled, 16)

            def root_of(norm, hf):
                act.wait_ge(made, 1)
                act.wait_ge(ssq, 2 * norm + hf + 1)
                nc.scalar.activation(rstd[:, hf * HALF:(hf + 1) * HALF], bank[NORM_BANK[hf]][:], ACT.Sqrt,
                                     scale=1.0 / D_MODEL, bias=eps[:, 0:1]).then_inc(root, 1)

            def ffn_step(i, f, last=False):
                step = i + FFN_STEPS * f
                unit = FFN_UNITS * i + (FFN2_0 if f else 0)
                later = isinstance(i, int) and i == 0 and not f
                first_step = isinstance(i, int) and i == 0
                for t in range(4):
                    tile, hf = t % 2, t // 2
                    act.wait_ge(gu_out, 8 * step + 2 * t + 1)
                    nc.scalar.activation(tmp[t % 2][:], tmp[t % 2][:], ACT.Silu).then_inc(silu_done, 1)
                    if t < 2:
                        before = None if later else (down_done, 16 * step + (DOWN_FFN2 - 16 * FFN_STEPS if f else 0))
                        split_high(unit + 4 + t, t % 2, 4 + t, before)
                    act.wait_ge(prod_done, 4 * step + t + 1)
                    nc.scalar.activation(gh[:, tile, hf * HALF:(hf + 1) * HALF], tmp[2 + t % 2][:], ACT.Copy).then_inc(g_high, 1)
                    if first_step and t == 0:
                        root_of(2 * f, 1)
                for j in range(4):
                    if last and f:
                        break
                    if last and j == 2:
                        for d in range(16):
                            prepare(1, d // 8, d % 8)
                    split_high(unit + FFN_UNITS + j, j % 2, j, (gu_done, 4 * step + 3 + j // 2))
                if last and f:
                    for d in range(8):
                        prepare(3, 0, d)
                    root_of(3, 0)
                    for d in range(8):
                        prepare(3, 1, d)
                    root_of(3, 1)
                elif last:
                    root_of(1, 0)

            split_high(0, 0, 0)
            for k in range(4):
                prepare(0, 0, k)
            split_high(1, 1, 1)
            for k in range(4, KT):
                prepare(0, 0, k)
            for j in range(2, 4):
                split_high(j, j % 2, j)
            root_of(0, 0)
            for k in range(KT):
                prepare(0, 1, k)
            ffn_step(0, 0)
            with act.Fori(1, FFN_STEPS - 1) as i:
                ffn_step(i, 0)
            ffn_step(FFN_STEPS - 1, 0, last=True)

            act.wait_ge(bias_scaled, 1)
            tiles = proj_tiles()
            for e in PLAN:
                if e[0] == "ssq":
                    root_of(1, 1)
                elif e[0] == "job":
                    n, hf = JOBS[e[1]]
                    role, u = tiles[n]
                    _, _, g = unit_of(u)
                    last_qk = {"q": 8 * (u - 1), "k": 8 * (u - 1)}.get(role)
                    act.wait_ge(job_scaled, e[1] + 1)
                    if e[1] == 0:
                        act.wait_ge(spilled, 16 * 16)
                    if hf == 0 and u >= 2 and role != "v":
                        act.wait_ge(qk_done, last_qk)
                    if hf == 0 and role == "v" and u:
                        act.wait_ge(m_done, M_INDEX[("m", "v", u - 1, 1)] + 1)
                    dst = {"q": qs[u % 2], "k": ks[u % 2], "v": vt}[role]
                    src = scaled[e[1] % 2][:] if g == 0 else scaled[e[1] % 2][:].rearrange("p (q r) -> p q r", r=DILATIONS[g])
                    nc.scalar.activation(fold(dst, g, hf), src, ACT.Identity, scale=HD ** -0.5 if role == "q" else 1.0,
                                         bias=(bias_q if role == "q" else bias_in)[:, n:n + 1]).then_inc(job_out, 1)
                    if hf:
                        split_high(PROJ_0 + n + RING, n % 2, n % RING, (job_done, e[1] + 1))
                elif e[0] == "qk":
                    c = e[1]
                    u, a, j = c // 4, c // 2 % 2, c % 2
                    act.wait_ge(negm_done, c + 1)
                    for i in range(4):
                        lo = 0 if has_previous(u, 4 * j + i) else P
                        last = nc.scalar.activation(sp[c % 2][:, i, lo:], sp[c % 2][:, i, lo:], ACT.Exp,
                                                    bias=negm[:, 4 * c + i:4 * c + i + 1],
                                                    accum_out=den[:, 4 * c + i:4 * c + i + 1])
                    if u >= A_UNITS:
                        head = u - A_UNITS + B_UNITS * a
                        s = 4 * (c - 4 * A_UNITS)
                        last = nc.scalar.activation(sexp[:, s:s + 4], negm[:, 4 * c:4 * c + 4], ACT.Exp, bias=sink[:, head:head + 1])
                    last.then_inc(exp_done, 1)
                elif e[0] == "t":
                    c = e[1]
                    act.wait_ge(t_done, 2 * c + 2)
                    dst, src = transposed(c, 1)
                    nc.scalar.activation(dst, src, ACT.Copy).then_inc(t_out[1], 1)
                elif e[0] == "mix" and e[1] == "exp":
                    for g in range(3):
                        act.wait_ge(mix_diff, 3 * e[2] + g + 1)
                        w = mix[e[2] // 2][g]
                        nc.scalar.activation(w[:], w[:], ACT.Exp).then_inc(mix_exp, 1)
                elif e[0] == "mix" and e[1] == "y":
                    pair, hf = e[2] // 2, e[2] % 2
                    act.wait_ge(mix_y, e[2] + 1)
                    nc.scalar.activation(yah[pair][:, hf * HALF:(hf + 1) * HALF], mix[pair][3][:], ACT.Copy).then_inc(ya_high, 1)
                elif e[:2] == ("m", "o") and e[2] >= A_UNITS:
                    i, hf = e[2] - A_UNITS, e[3]
                    act.wait_ge(m_done, M_INDEX[e] + 1)
                    if i >= 2:
                        act.wait_ge(y_low, 4)
                    nc.scalar.activation(ybh[i][:, hf * HALF:(hf + 1) * HALF], bank[7][:], ACT.Copy).then_inc(yb_high, 1)
                elif e[:2] == ("m", "stat"):
                    pair = e[2]
                    act.wait_ge(pv_out, 4 * (3 * pair + 2) + 4)
                    if pair:
                        act.wait_ge(m_done, M_INDEX[("m", "stat", 0)] + 1)
                    nc.scalar.activation(lse[:].rearrange("p g c -> p (g c)"), den[:, 48 * pair:48 * pair + 48], ACT.Ln).then_inc(ln_done, 1)

            def merge_step(i, last=False):
                unit = MERGE_0 + MERGE_UNITS * i
                nc.scalar.activation(gate_bias[:], bias_in[:, bass.ds(PROJ + 4 * i, 4)], ACT.Copy).then_inc(gate_bias_set, 1)
                act.wait_ge(gate_bias_set, i + 1)
                for t in range(4):
                    tile, hf = t // 2, t % 2
                    job = 4 * i + t
                    for gate in range(2):
                        act.wait_ge(mul_done, 5 * job + 2 * gate + 1)
                        nc.scalar.activation(tmp[gate][:], tmp[gate][:], ACT.Sigmoid,
                                             bias=gate_bias[:, 2 * tile + gate:2 * tile + gate + 1]).then_inc(sig_done, 1)
                        if hf:
                            j = 3 * tile + gate + RING
                            split_high(unit + j, j % 2, j % RING, (part_done, 4 * job + 2 * gate + 1))
                    act.wait_ge(mul_done, 5 * job + 5)
                    nc.scalar.activation(gh[:, tile, hf * HALF:(hf + 1) * HALF], tmp[2][:], ACT.Copy).then_inc(m_high, 1)
                    if hf:
                        j = 3 * tile + 2 + RING
                        split_high(unit + j, j % 2, j % RING, (part_done, 4 * job + 4))
                if last:
                    for d in range(16):
                        prepare(2, d // 8, d % 8)
                for j in range(2):
                    split_high(unit + 10 + j, j % 2, 2 + j, (down_done, DOWN_MERGE + 16 * i + 16))

            act.wait_ge(m_out, len(M_EVENTS))
            act.wait_ge(spilled, 16 * 16)
            act.dma_start(h[:], h_spill[:, :, :]).then_inc(h_back, 16)
            with act.Fori(0, MERGE_STEPS - 1) as i:
                merge_step(i)
            merge_step(MERGE_STEPS - 1, last=True)
            root_of(2, 0)
            ffn_step(0, 1)
            with act.Fori(1, FFN_STEPS - 1) as i:
                ffn_step(i, 1)
            ffn_step(FFN_STEPS - 1, 1, last=True)

        @block.vector
        def _(dve):
            def split_low(u, parity, slot):
                dve.wait_ge(w_high, u + 1)
                nc.vector.tensor_tensor(wl[slot][:], raw[parity][:], wh[slot][:], ALU.subtract).then_inc(w_low, 1)

            def low(norm, hf, k):
                cols = slice(hf * HALF, (hf + 1) * HALF)
                dve.wait_ge(x_high, 16 * norm + 8 * hf + k + 1)
                nc.vector.scalar_tensor_tensor(out=xl[:, k, cols], in0=h[:, k, cols], scalar=gain[:, norm, k:k + 1],
                                               in1=xh[:, k, cols], op0=ALU.mult, op1=ALU.subtract).then_inc(x_low, 1)

            def invert(norm, hf):
                cols = slice(hf * HALF, (hf + 1) * HALF)
                dve.wait_ge(root, 2 * norm + hf + 1)
                nc.vector.reciprocal(rstd[:, cols], rstd[:, cols]).then_inc(rstd_done, 1)
                dve.wait_ge(rstd_done, 2 * norm + hf + 1)

            def result(hf, k):
                cols = slice(hf * HALF, (hf + 1) * HALF)
                nc.vector.scalar_tensor_tensor(out=h[:, k, cols], in0=h[:, k, cols], scalar=gain[:, 3, k:k + 1],
                                               in1=rstd[:, cols], op0=ALU.mult, op1=ALU.mult).then_inc(x_out, 1)

            def ffn_step(i, f, last=False):
                step = i + FFN_STEPS * f
                unit = FFN_UNITS * i + (FFN2_0 if f else 0)
                first_step = isinstance(i, int) and i == 0
                for t in range(4):
                    tile, hf = t % 2, t // 2
                    cols = slice(hf * HALF, (hf + 1) * HALF)
                    dve.wait_ge(gu_done, 4 * step + t + 1)
                    if not (first_step and not f and t < 2):
                        dve.wait_ge(g_low, 4 * step + t - 1)
                    for part in range(2):
                        nc.vector.tensor_tensor(tmp[2 * part + t % 2][:], bank[2 * (t % 2) + part][:], rstd[:, cols], ALU.mult).then_inc(gu_out, 1)
                    if t < 2:
                        split_low(unit + 4 + t, t % 2, 4 + t)
                    dve.wait_ge(gu_out, 8 * step + 2 * t + 2)
                    dve.wait_ge(silu_done, 4 * step + t + 1)
                    nc.vector.tensor_tensor(tmp[2 + t % 2][:], tmp[t % 2][:], tmp[2 + t % 2][:], ALU.mult).then_inc(prod_done, 1)
                    dve.wait_ge(g_high, 4 * step + t + 1)
                    nc.vector.tensor_tensor(gl[:, tile, cols], tmp[2 + t % 2][:], gh[:, tile, cols], ALU.subtract).then_inc(g_low, 1)
                    if first_step and t == 0:
                        invert(2 * f, 1)
                first = 16 * step + (DOWN_FFN2 - 16 * FFN_STEPS if f else 0)
                for d in range(16):
                    hf, k = d // 8, d % 8
                    cols = slice(hf * HALF, (hf + 1) * HALF)
                    dve.wait_ge(down_done, first + d + 1)
                    nc.vector.scalar_tensor_tensor(out=h[:, k, cols], in0=bank[4 + d % 4][:], scalar=0.5, in1=h[:, k, cols],
                                                   op0=ALU.mult, op1=ALU.add).then_inc(down_added, 1)
                    if last and not f:
                        if d in (1, 3):
                            split_low(unit + FFN_UNITS + d // 2, d // 2, d // 2)
                        if d:
                            low(1, (d - 1) // 8, (d - 1) % 8)
                    elif last and d == 12:
                        invert(3, 0)
                    elif d % 4 == 1 and not last:
                        split_low(unit + FFN_UNITS + d // 4, d // 4 % 2, d // 4)
                if last and not f:
                    low(1, 1, KT - 1)
                    for j in range(2, 4):
                        split_low(unit + FFN_UNITS + j, j % 2, j)
                    invert(1, 0)
                elif last:
                    for k in range(KT):
                        result(0, k)
                    invert(3, 1)
                    for k in range(KT):
                        result(1, k)

            dve.wait_ge(const_in, 48)
            split_low(0, 0, 0)
            for k in range(4):
                low(0, 0, k)
            split_low(1, 1, 1)
            for k in range(4, KT):
                low(0, 0, k)
            for j in range(2, 4):
                split_low(j, j % 2, j)
            for v, n in enumerate((4, 4, 4, 8)):
                dve.wait_ge(vec_done, v + 1)
                nc.vector.tensor_copy(rows[0:n, v, :], bank[4 + v][0:n, 0:VEC]).then_inc(vec_out, 1)
            invert(0, 0)
            for k in range(KT):
                low(0, 1, k)
            nc.vector.tensor_scalar(bias_q[:], bias_in[:], HD ** -0.5, None, ALU.mult).then_inc(bias_scaled, 1)
            ffn_step(0, 0)
            with dve.Fori(1, FFN_STEPS - 1) as i:
                ffn_step(i, 0)
            ffn_step(FFN_STEPS - 1, 0, last=True)

            for e in PLAN:
                if e[0] == "ssq":
                    invert(1, 1)
                elif e[0] == "job":
                    n, hf = JOBS[e[1]]
                    dve.wait_ge(job_done, e[1] + 1)
                    if e[1] == 0:
                        dve.wait_ge(sq_sum, 4 * (KT - 1))
                    if e[1] >= 2:
                        dve.wait_ge(job_out, e[1] - 1)
                    nc.vector.tensor_tensor(scaled[e[1] % 2][:], bank[e[1] % 2][:], rstd[:, hf * HALF:(hf + 1) * HALF],
                                            ALU.mult).then_inc(job_scaled, 1)
                    if hf:
                        split_low(PROJ_0 + n + RING, n % 2, n % RING)
                elif e[0] == "qk":
                    c = e[1]
                    u, a, j = c // 4, c // 2 % 2, c % 2
                    kind, pair, g = unit_of(u)
                    for i in range(4):
                        lo = 0 if has_previous(u, 4 * j + i) else P
                        if i % 2 == 0:
                            dve.wait_ge(qk_done, 2 * c + i // 2 + 1)
                        head = pair + B_UNITS * a if kind == "B" else A_SLOTS * g + 2 * pair + a
                        bias = bias_B[:, head, lo:] if kind == "B" else bias_A[:, head, lo:] if g < 2 else bias_2[:, head - 2 * A_SLOTS, :]
                        nc.vector.tensor_tensor_reduce(out=sp[c % 2][:, i, lo:], in0=bank[2 + i // 2][:, i % 2 * 2 * P + lo:(i % 2 + 1) * 2 * P],
                                                       in1=bias, scale=1.0, scalar=3 * NEG, op0=ALU.add, op1=ALU.max,
                                                       accum_out=rmax[:, c % 2, i:i + 1]).then_inc(max_done, 1)
                    dve.wait_ge(max_done, 4 * c + 4)
                    floor = sink[:, head:head + 1] if kind == "B" else 3 * NEG
                    nc.vector.tensor_scalar(negm[:, 4 * c:4 * c + 4], rmax[:, c % 2, :], floor, -1.0, ALU.max, ALU.mult).then_inc(negm_done, 1)
                elif e[0] == "t":
                    c = e[1]
                    dve.wait_ge(t_done, 2 * c + 1)
                    dst, src = transposed(c, 0)
                    nc.vector.tensor_copy(dst, src).then_inc(t_out[0], 1)
                elif e[0] == "mix":
                    n = e[2]
                    pair, hf = n // 2, n % 2
                    if e[1] == "inv":
                        dve.wait_ge(mix_sum, 2 * n + 2)
                        nc.vector.reciprocal(mix[pair][3][:], mix[pair][3][:]).then_inc(mix_inv, 1)
                    elif e[1] == "y":
                        cols = slice(hf * HALF, (hf + 1) * HALF)
                        dve.wait_ge(ya_high, n + 1)
                        nc.vector.tensor_tensor(yal[pair][:, cols], mix[pair][3][:], yah[pair][:, cols], ALU.subtract).then_inc(y_low, 1)
                elif e[0] == "pv":
                    c = e[1]
                    u, a, j = c // 4, c // 2 % 2, c % 2
                    total = den[:, 4 * c:4 * c + 4]
                    dve.wait_ge(pv_done, c + 1)
                    if u >= A_UNITS:
                        s = 4 * (c - 4 * A_UNITS)
                        nc.vector.tensor_tensor(total, total, sexp[:, s:s + 4], ALU.add).then_inc(den_done, 1)
                        dve.wait_ge(den_done, c + c - 4 * A_UNITS + 1)
                    nc.vector.reciprocal(rden[:, c % 2, :], total).then_inc(den_done, 1)
                    dve.wait_ge(den_done, c + 1 + max(0, c - 4 * A_UNITS + 1))
                    nc.vector.tensor_tensor(ob[:, 4 * j:4 * j + 4, a * HD:(a + 1) * HD],
                                            bank[6][:, 0:4 * HD].rearrange("p (i d) -> p i d", i=4),
                                            rden[:, c % 2, :].unsqueeze(2).to_broadcast([P, 4, HD]), ALU.mult).then_inc(pv_out, 1)
                else:
                    m = M_INDEX[e]
                    if e[1] == "stat":
                        pair = e[2]
                        dve.wait_ge(ln_done, pair + 1)
                        flat = lse[:].rearrange("p g c -> p (g c)")
                        nc.vector.tensor_tensor(flat, flat, negm[:, 48 * pair:48 * pair + 48], ALU.subtract).then_inc(lse_made, 1)
                    dve.wait_ge(m_done, m + 1)
                    if e[1] == "bias":
                        n = e[2]
                        src = bank[7][:].rearrange("p (h k) -> p h k", h=2)
                        if n < 4:
                            nc.vector.tensor_copy(bias_A[:, 2 * n:2 * n + 2, :], src).then_inc(m_out, 1)
                        elif n < 6:
                            nc.vector.tensor_copy(bias_2[:, 2 * n - 8:2 * n - 6, :], src[:, :, P:]).then_inc(m_out, 1)
                            if n == 5:
                                dve.wait_ge(m_out, m + 1)
                                nc.vector.memset(bias_2[HD:, :, 0:HD], NEG).then_inc(mask_set, 1)
                                dve.wait_ge(mask_set, 1)
                        else:
                            nc.vector.tensor_copy(bias_B[:, 2 * n - 12:2 * n - 10, :], src).then_inc(m_out, 1)
                    elif e[1] == "v":
                        u, hf = e[2], e[3]
                        nc.vector.tensor_copy(vs[u % 2][:, 4 * hf:4 * hf + 4, :], bank[7][:].rearrange("p (i d) -> p i d", i=4)).then_inc(m_out, 1)
                    elif e[1] == "o":
                        u, hf = e[2], e[3]
                        kind, i, g = unit_of(u)
                        if kind == "A":
                            dst = unfold(og[u % 4], g, hf)
                            if u >= 4:
                                dve.wait_ge(mix_y, 2)
                            src = bank[7][:]
                            if g == 1:
                                src = src.rearrange("p (r b q) -> p r b q", r=2, b=2)
                            elif g == 2:
                                src = src.rearrange("p (r j) -> p r j", r=8)
                            nc.vector.tensor_copy(dst, src).then_inc(m_out, 1)
                        else:
                            cols = slice(hf * HALF, (hf + 1) * HALF)
                            dve.wait_ge(yb_high, 2 * i + hf + 1)
                            nc.vector.tensor_tensor(ybl[i][:, cols], bank[7][:], ybh[i][:, cols], ALU.subtract).then_inc(m_out, 1)
                    elif e[1] == "stat":
                        nc.vector.tensor_copy(lseT[:].rearrange("k g q -> k (g q)"), bank[7][0:16, 0:3 * P]).then_inc(m_out, 1)
                    elif e[1] == "lse":
                        pair, hf, g = e[2:]
                        nc.vector.tensor_copy(mix[pair][g][:], bank[7][:]).then_inc(m_out, 1)
                        if g == 2:
                            top, n = mix[pair][3], 2 * pair + hf
                            dve.wait_ge(m_out, m + 1)
                            if n:
                                dve.wait_ge(y_low, n)
                            nc.vector.tensor_tensor(top[:], mix[pair][0][:], mix[pair][1][:], ALU.max).then_inc(mix_top, 1)
                            dve.wait_ge(mix_top, 2 * n + 1)
                            nc.vector.tensor_tensor(top[:], top[:], mix[pair][2][:], ALU.max).then_inc(mix_top, 1)

            def merge_step(i, last=False):
                unit = MERGE_0 + MERGE_UNITS * i
                for t in range(4):
                    tile, hf = t // 2, t % 2
                    job = 4 * i + t
                    cols = slice(hf * HALF, (hf + 1) * HALF)
                    if not (isinstance(job, int) and job == 0):
                        dve.wait_ge(m_low, job)
                    for gate in range(2):
                        dve.wait_ge(part_done, 4 * job + 2 * gate + 1)
                        if not (isinstance(job, int) and job == 0):
                            dve.wait_ge(mul_done, 5 * job)
                        nc.vector.tensor_tensor(tmp[gate][:], bank[2 * gate][:], rstd[:, cols], ALU.mult).then_inc(mul_done, 1)
                        dve.wait_ge(sig_done, 2 * job + gate + 1)
                        dve.wait_ge(part_done, 4 * job + 2 * gate + 2)
                        nc.vector.tensor_tensor(tmp[gate][:], tmp[gate][:], bank[2 * gate + 1][:], ALU.mult).then_inc(mul_done, 1)
                        if hf:
                            j = 3 * tile + gate + RING
                            split_low(unit + j, j % 2, j % RING)
                    dve.wait_ge(mul_done, 5 * job + 4)
                    nc.vector.tensor_tensor(tmp[2][:], tmp[0][:], tmp[1][:], ALU.add).then_inc(mul_done, 1)
                    dve.wait_ge(m_high, job + 1)
                    nc.vector.tensor_tensor(gl[:, tile, cols], tmp[2][:], gh[:, tile, cols], ALU.subtract).then_inc(m_low, 1)
                    if hf:
                        j = 3 * tile + 2 + RING
                        split_low(unit + j, j % 2, j % RING)
                first = DOWN_MERGE + 16 * i
                for d in range(16):
                    hf, k = d // 8, d % 8
                    cols = slice(hf * HALF, (hf + 1) * HALF)
                    dve.wait_ge(down_done, first + d + 1)
                    nc.vector.tensor_tensor(h[:, k, cols], bank[4 + d % 4][:], h[:, k, cols], ALU.add).then_inc(down_added, 1)
                    if last and d:
                        low(2, (d - 1) // 8, (d - 1) % 8)
                if last:
                    low(2, 1, KT - 1)
                for j in range(2):
                    split_low(unit + 10 + j, j % 2, 2 + j)

            dve.wait_ge(h_back, 16)
            with dve.Fori(0, MERGE_STEPS - 1) as i:
                merge_step(i)
            merge_step(MERGE_STEPS - 1, last=True)
            invert(2, 0)
            ffn_step(0, 1)
            with dve.Fori(1, FFN_STEPS - 1) as i:
                ffn_step(i, 1)
            ffn_step(FFN_STEPS - 1, 1, last=True)

        @block.tensor
        def _(pe):
            def product(out, slot, col, moving, first, last):
                hi, lo = moving
                cols = slice(col * P, (col + 1) * P)
                nc.tensor.matmul(out, wh[slot][:, cols], hi, start=first, stop=False)
                nc.tensor.matmul(out, wh[slot][:, cols], lo, start=False, stop=False)
                return nc.tensor.matmul(out, wl[slot][:, cols], hi, start=False, stop=last)

            def normed(k, hf):
                cols = slice(hf * HALF, (hf + 1) * HALF)
                return xh[:, k, cols], xl[:, k, cols]

            def gated(t, hf):
                cols = slice(hf * HALF, (hf + 1) * HALF)
                return gh[:, t, cols], gl[:, t, cols]

            def project(out, slot, hf, norm=None):
                for k in range(KT):
                    if norm is not None:
                        pe.wait_ge(x_low, 16 * norm + 8 * hf + k + 1)
                    last = product(out, slot, k, normed(k, hf), k == 0, k == KT - 1)
                return last

            def sum_squares(norm, hf):
                pe.wait_ge(made, 2)
                pe.wait_ge(sq_sum, (KT - 1) * (2 * norm + hf + 1))
                nc.tensor.matmul(bank[NORM_BANK[hf]][:], ones[:], acc[hf][:], start=True, stop=True).then_inc(ssq, 1)

            def distance_biases():
                pe.wait_ge(made, 5)
                pe.wait_ge(tab_in, 32)
                for v, (first, n) in enumerate(((0, 4), (4, 4), (8, 4), (12, 8))):
                    nc.tensor.matmul(bank[4 + v][0:n, 0:VEC], tab[:, first:first + n], hot[:, v, :], start=True, stop=True).then_inc(vec_done, 1)

            def ffn_step(i, f, last=False):
                step = i + FFN_STEPS * f
                unit = FFN_UNITS * i + (FFN2_0 if f else 0)
                first_step = isinstance(i, int) and i == 0
                for t in range(4):
                    tile, hf = t % 2, t // 2
                    if not (first_step and t < 2 and not f):
                        pe.wait_ge(gu_out, 8 * step + 2 * t - 2)
                    if first_step and t == 1:
                        pe.wait_ge(root, 4 * f + 1)
                    norm = 2 * f if first_step and tile == 0 else None
                    for part in range(2):
                        if hf == 0:
                            pe.wait_ge(w_low, unit + 2 * tile + part + 1)
                        done = project(bank[2 * (t % 2) + part][:], 2 * tile + part, hf, norm if part == 0 else None)
                    done.then_inc(gu_done, 1)
                    if first_step and t == 0:
                        if not f:
                            distance_biases()
                        sum_squares(2 * f, f)
                    if first_step and t == 1 and not f:
                        pe.wait_ge(vec_out, 1)
                        sum_squares(0, 1)
                first = 16 * step + (DOWN_FFN2 - 16 * FFN_STEPS if f else 0)
                pe.wait_ge(w_low, unit + 6)
                for d in range(16):
                    hf, k = d // 8, d % 8
                    if k == 0:
                        pe.wait_ge(g_low, 4 * step + 2 * hf + 2)
                    if not (first_step and not f and d < 4):
                        pe.wait_ge(down_added, first + d - 3)
                    for t in range(2):
                        done = product(bank[4 + d % 4][:], 4 + t, k, gated(t, hf), t == 0, t == 1)
                    done.then_inc(down_done, 1)
                    if last and d == (11 if f else 15):
                        sum_squares(1 + 2 * f, 0)

            ffn_step(0, 0)
            with pe.Fori(1, FFN_STEPS - 1) as i:
                ffn_step(i, 0)
            ffn_step(FFN_STEPS - 1, 0, last=True)

            tiles = proj_tiles()
            for e in PLAN:
                if e[0] == "mix":
                    continue
                if e[0] == "ssq":
                    sum_squares(1, 1)
                elif e[0] == "job":
                    n, hf = JOBS[e[1]]
                    if hf == 0:
                        pe.wait_ge(w_low, PROJ_0 + n + 1)
                    if e[1] >= 2:
                        pe.wait_ge(job_scaled, e[1] - 1)
                    project(bank[e[1] % 2][:], n % RING, hf, 1 if n == 0 else None).then_inc(job_done, 1)
                elif e[0] == "qk":
                    c = e[1]
                    u, a, j = c // 4, c // 2 % 2, c % 2
                    q_tile, k_tile = tiles.index(("q", u)), tiles.index(("k", min(u, A_UNITS)))
                    q, k = qs[u % 2], ks[min(u, A_UNITS) % 2]
                    part = slice(a * HD, (a + 1) * HD)
                    pe.wait_ge(job_out, JOB_INDEX[(max(q_tile, k_tile), 1)] + 1)
                    for i in range(4):
                        tile = 4 * j + i
                        lo = 0 if has_previous(u, tile) else P
                        if c and i % 2 == 0:
                            pe.wait_ge(max_done, 4 * (c - 1) + 2 * (i // 2) + 2)
                        last = nc.tensor.matmul(bank[2 + i // 2][:, i % 2 * 2 * P + lo:(i % 2 + 1) * 2 * P],
                                                q[part, tile * P:(tile + 1) * P],
                                                k[part, (tile - 1) * P + lo:(tile + 1) * P], start=True, stop=True)
                        if i % 2:
                            last.then_inc(qk_done, 1)
                elif e[0] == "t":
                    c = e[1]
                    u, j = c // 4, c % 2
                    pe.wait_ge(exp_done, c + 1)
                    for i in range(4):
                        if c and i % 2 == 0:
                            pe.wait_ge(t_out[i // 2], c)
                        for b in range(0 if has_previous(u, 4 * j + i) else 1, 2):
                            last = nc.tensor.transpose(bank[4 + i // 2][:, (i % 2 * 2 + b) * P:(i % 2 * 2 + b + 1) * P],
                                                       sp[c % 2][:, i, b * P:(b + 1) * P], ident[:])
                        if i % 2:
                            last.then_inc(t_done, 1)
                elif e[0] == "pv":
                    c = e[1]
                    u, a, j = c // 4, c // 2 % 2, c % 2
                    vu = min(u, A_UNITS)
                    pe.wait_ge(m_out, M_INDEX[("m", "v", vu, 1)] + 1)
                    pe.wait_ge(t_out[0], c + 1)
                    pe.wait_ge(t_out[1], c + 1)
                    if c:
                        pe.wait_ge(pv_out, c)
                    for i in range(4):
                        tile = 4 * j + i
                        start = 0 if has_previous(u, tile) else 1
                        for b in range(start, 2):
                            last = nc.tensor.matmul(bank[6][:, i * HD:(i + 1) * HD], pt[c % 2][:, i, b * P:(b + 1) * P],
                                                    vs[vu % 2][:, tile - 1 + b, a * HD:(a + 1) * HD], start=b == start, stop=b == 1)
                    last.then_inc(pv_done, 1)
                else:
                    m = M_INDEX[e]
                    if m:
                        pe.wait_ge(m_out, m)
                    if e[1] == "bias":
                        if e[2] == 0:
                            pe.wait_ge(skew_in, 16)
                            pe.wait_ge(made, 7)
                        last = nc.tensor.matmul(bank[7][:], flip[:], skew[:, 2 * e[2]:2 * e[2] + 2, :].rearrange("p h k -> p (h k)"),
                                                start=True, stop=True)
                    elif e[1] == "v":
                        u, hf = e[2], e[3]
                        pe.wait_ge(job_out, JOB_INDEX[(tiles.index(("v", u)), 1)] + 1)
                        for i in range(4):
                            last = nc.tensor.transpose(bank[7][:, i * P:(i + 1) * P], vt[:, (4 * hf + i) * P:(4 * hf + i + 1) * P], ident[:])
                    elif e[1] == "o":
                        u, hf = e[2], e[3]
                        pe.wait_ge(pv_out, 4 * u + 4)
                        for i in range(4):
                            last = nc.tensor.transpose(bank[7][:, i * P:(i + 1) * P], ob[:, 4 * hf + i, :], ident[:])
                    elif e[1] == "stat":
                        pe.wait_ge(lse_made, e[2] + 1)
                        for g in range(3):
                            last = nc.tensor.transpose(bank[7][0:16, g * P:(g + 1) * P], lse[:, g, :], ident[:])
                    else:
                        _, _, pair, hf, g = e
                        pe.wait_ge(sel_made, 2)
                        for i in range(4 if g < 2 else 8):
                            tile = 4 * hf + i if g == 0 else 2 * i + hf if g == 1 else i
                            src = lseT[:, g, :]
                            if g == 0:
                                out = bank[7][:, i * P:(i + 1) * P]
                            elif g == 1:
                                out = bank[7][:].rearrange("p (q r) -> p r q", r=4)[:, i, :]
                            else:
                                src = src.rearrange("k (s j) -> k s j", s=2)[:, :, 32 * hf:32 * hf + 32]
                                out = bank[7][:].rearrange("p (j r) -> p r j", r=16)[:, 2 * i:2 * i + 2, :]
                            last = nc.tensor.matmul(out, sel[:, tile, :], src, start=True, stop=True)
                    last.then_inc(m_done, 1)

            def merge_step(i, last=False):
                unit = MERGE_0 + MERGE_UNITS * i
                first_step = isinstance(i, int) and i == 0
                for t in range(4):
                    tile, hf = t // 2, t % 2
                    job = 4 * i + t
                    cols = slice(hf * HALF, (hf + 1) * HALF)
                    for part in range(4):
                        gate = part // 2
                        if hf == 0 and part != 3:
                            pe.wait_ge(w_low, unit + 3 * tile + (0, 2, 1)[part] + 1 if part != 1 else unit + 3 * tile + 3)
                        if not (first_step and t == 0):
                            pe.wait_ge(mul_done, 5 * job - 4 + part)
                        slot = (3 * tile + gate) % RING
                        if part % 2 == 0:
                            done = project(bank[part][:], slot, hf)
                        else:
                            slot = (3 * tile + 2) % RING
                            ys = [(yah[p], yal[p]) for p in range(2)] if gate == 0 else [(ybh[p], ybl[p]) for p in range(B_UNITS)]
                            for p, (hi, lo) in enumerate(ys):
                                done = product(bank[part][:], slot, 2 * gate + p, (hi[:, cols], lo[:, cols]), p == 0, p == len(ys) - 1)
                        done.then_inc(part_done, 1)
                pe.wait_ge(w_low, unit + 8)
                first = DOWN_MERGE + 16 * i
                for d in range(16):
                    hf, k = d // 8, d % 8
                    if k == 0:
                        pe.wait_ge(m_low, 4 * i + 3 + hf)
                    pe.wait_ge(down_added, first + d - 3)
                    for t in range(2):
                        done = product(bank[4 + d % 4][:], 2 + t, k, gated(t, hf), t == 0, t == 1)
                    done.then_inc(down_done, 1)
                    if last and d == 15:
                        sum_squares(2, 0)

            pe.wait_ge(job_scaled, 2 * PROJ)
            pe.wait_ge(max_done, 4 * CHUNKS)
            pe.wait_ge(pv_out, CHUNKS)
            pe.wait_ge(m_out, len(M_EVENTS))
            merge_step(0)
            with pe.Fori(1, MERGE_STEPS - 1) as i:
                merge_step(i)
            merge_step(MERGE_STEPS - 1, last=True)
            ffn_step(0, 1)
            with pe.Fori(1, FFN_STEPS - 1) as i:
                ffn_step(i, 1)
            ffn_step(FFN_STEPS - 1, 1, last=True)
            sum_squares(3, 1)


NORM_BANK = (3, 4)


def kernel(x, ffn1_norm, ffn1_w_gate, ffn1_w_up, ffn1_w_down, mix_norm, w_in, b_in, w_branch_a, w_branch_b, w_out,
           sinks, rel_bias, ffn2_norm, ffn2_w_gate, ffn2_w_up, ffn2_w_down, final_norm):
    import concourse.bacc as bacc
    from concourse.bass_utils import run_bass_kernel_spmd

    stream = np.zeros((N_UNITS, P, UNIT), np.float32)
    at = iter(range(N_UNITS))

    def columns(w, cols):
        stream[next(at)] = w[:, cols].reshape(KT, P, P).transpose(1, 0, 2).reshape(P, UNIT)

    def ffn(gate, up, down):
        for i in range(FFN_STEPS):
            for t in (2 * i, 2 * i + 1):
                columns(gate, np.arange(t * P, (t + 1) * P))
                columns(up, np.arange(t * P, (t + 1) * P))
            for t in (2 * i, 2 * i + 1):
                stream[next(at)] = down[t * P:(t + 1) * P, :]

    w = np.asarray(w_in[0])
    b = np.asarray(b_in[0])
    ffn(np.asarray(ffn1_w_gate[0]), np.asarray(ffn1_w_up[0]), np.asarray(ffn1_w_down[0]))
    order = [head_columns(role, u) for role, u in proj_tiles()]
    for cols in order:
        columns(w, cols)
    gates = D_IN - 2 * D_MODEL
    wa, wo = np.asarray(w_branch_a[0]), np.asarray(w_out[0])
    wb = np.asarray(w_branch_b[0]).reshape(2, B_UNITS, HD, D_MODEL).transpose(1, 0, 2, 3).reshape(B_HEADS * HD, D_MODEL)
    for i in range(MERGE_STEPS):
        for t in (2 * i, 2 * i + 1):
            pair = [np.arange(gates + g * D_MODEL + t * P, gates + g * D_MODEL + (t + 1) * P) for g in range(2)]
            order += pair
            for cols in pair:
                columns(w, cols)
            both = np.concatenate([wa, wb])[:, t * P:(t + 1) * P].reshape(6, P, P).transpose(1, 0, 2).reshape(P, 6 * P)
            stream[next(at), :, 0:6 * P] = both
        for t in (2 * i, 2 * i + 1):
            stream[next(at)] = wo[t * P:(t + 1) * P, :]
    ffn(np.asarray(ffn2_w_gate[0]), np.asarray(ffn2_w_up[0]), np.asarray(ffn2_w_down[0]))

    norms = [np.asarray(ffn1_norm[0]), np.asarray(mix_norm[0]), np.asarray(ffn2_norm[0]), np.asarray(final_norm)]
    arrays = {
        "xT": np.ascontiguousarray(np.asarray(x[0]).T),
        "stream": stream,
        "gains": np.ascontiguousarray(np.stack(norms).reshape(4, KT, P).transpose(2, 0, 1)),
        "b_in": np.ascontiguousarray(np.stack([b[c] for c in order]).T),
        "sinks": np.ascontiguousarray(np.asarray(sinks[0])),
        "rel_bias": np.ascontiguousarray(np.asarray(rel_bias)),
        "onehot": distance_onehot(),
    }
    nc = bacc.Bacc("TRN2", target_bir_lowering=False, num_devices=1, dynamic_dma_scratch_size=4096)
    args = [nc.dram_tensor(n, a.shape, mybir.dt.from_np(a.dtype), kind="ExternalInput").ap() for n, a in arrays.items()]
    bias_rows = nc.dram_tensor("bias_rows", (HEADS, VEC), mybir.dt.float32, kind="Internal").ap()
    h_spill = nc.dram_tensor("h_spill", (P, KT, SEQ), mybir.dt.float32, kind="Internal").ap()
    outT = nc.dram_tensor("outT", (D_MODEL, SEQ), mybir.dt.float32, kind="ExternalOutput").ap()
    build(nc, *args, bias_rows, h_spill, outT)
    r = run_bass_kernel_spmd(nc, [arrays], core_ids=[0])
    return np.ascontiguousarray(r.results[0]["outT"].T)[None]
```

```python
import math
from contextlib import ExitStack

import numpy as np

import concourse.bass as bass
from concourse import mybir

P = 128
D_MODEL, SEQ, D_FF = 1024, 1024, 2816
HD = 64
EPS = 1e-6
DILATIONS = (1, 4, 16)
WINDOWS = (128, 512, 2048)
A_SLOTS = 4
A_HEADS, B_HEADS, B_KV = 12, 8, 2
B_WINDOW = 128
N_BUCKETS, MAX_DISTANCE = 32, 2048
HEADS = A_HEADS + B_HEADS
D_IN = 3 * A_HEADS * HD + B_HEADS * HD + 2 * B_KV * HD + 2 * D_MODEL

KT = D_MODEL // P
HALF = SEQ // 2
FT = D_FF // P
FFN_STEPS = FT // 2
UNIT = 1024
FFN_UNITS = 6
A_UNITS = 6
B_UNITS = 4
HEAD_UNITS = A_UNITS + B_UNITS
PROJ = 3 * A_UNITS + 2 + B_UNITS
MERGE_STEPS = KT // 2
MERGE_UNITS = 8
PROJ_0 = FFN_UNITS * FFN_STEPS
MERGE_0 = PROJ_0 + PROJ
FFN2_0 = MERGE_0 + MERGE_UNITS * MERGE_STEPS
N_UNITS = FFN2_0 + FFN_UNITS * FFN_STEPS
RING = 4
CHUNKS = 4 * HEAD_UNITS
QT = SEQ // P
BIN_TILES = D_IN // P
T_LAG, PV_LAG = 2, 3
NEG = -1e30
VEC = 384



def unit_of(u):
    return ("A", u // 3, u % 3) if u < A_UNITS else ("B", u - A_UNITS, 0)


def proj_tiles():
    out = []
    for u in range(A_UNITS + 1):
        out += [("q", u), ("k", u), ("v", u)]
    return out + [("q", u) for u in range(A_UNITS + 1, HEAD_UNITS)]


def head_columns(role, u):
    kind, a, g = unit_of(u)
    qa, qb = 0, 3 * A_HEADS * HD
    if kind == "A":
        at = {"q": 0, "k": 1, "v": 2}[role] * A_HEADS * HD + (A_SLOTS * g + 2 * a) * HD
        return np.arange(at, at + P)
    if role == "q":
        return np.concatenate([np.arange(qb + h * HD, qb + (h + 1) * HD) for h in (a, a + B_HEADS // 2)])
    at = qb + B_HEADS * HD + (0 if role == "k" else B_KV * HD)
    return np.arange(at, at + P)


def bucket(dist):
    max_exact = N_BUCKETS // 2
    n = np.maximum(dist, 0)
    nf = np.maximum(n, 1).astype(np.float32)
    large = max_exact + (np.log(nf / np.float32(max_exact)) / np.float32(math.log(MAX_DISTANCE / max_exact))
                         * np.float32(N_BUCKETS - max_exact)).astype(np.int32)
    return np.where(n < max_exact, n, np.minimum(large, N_BUCKETS - 1))


def distance_onehot():
    out = np.zeros((N_BUCKETS + 1, 4, VEC), np.float32)
    steps = [(d, w // d) for w, d in zip(WINDOWS, DILATIONS)] + [(1, B_WINDOW - 1)]
    for v, (d, most) in enumerate(steps):
        for j in range(VEC):
            dist = 2 * P - 1 - j
            row = int(bucket(np.array(dist * d))) if 0 <= dist <= most else N_BUCKETS
            out[row, v, j] = 1.0
    return out


JOBS = [(n, hf) for hf in range(2) for n in range(2)] + [(n, hf) for n in range(2, PROJ) for hf in range(2)]
JOB_INDEX = {job: j for j, job in enumerate(JOBS)}


def attention_plan():
    plan = []
    jobs = iter(range(2 * PROJ))

    used = []

    def job(n=1):
        for _ in range(n):
            plan.append(("job", next(jobs)))
            tile, hf = JOBS[plan[-1][1]]
            used.extend([tile] * hf)

    def refill():
        plan.extend(("w", used.pop(0)) for _ in range(len(used)))

    job(2)
    plan.append(("ssq",))
    job(2)
    refill()
    for i in range(HEADS // 2):
        plan.append(("m", "bias", i))
        if i in (3, 7):
            job()
    refill()
    for u in range(HEAD_UNITS + 1):
        for s in range(4):
            c = 4 * u + s
            if c < CHUNKS:
                plan.append(("qk", c))
            n_jobs = (1, 2, 1, 2)[s] if u < A_UNITS else (0, 1, 0, 1)[s] if u < HEAD_UNITS - 1 else 0
            if n_jobs:
                job()
            done = {4: 0, 5: 1, 7: 2, 8: 3}.get(u)
            misc = []
            if s == 1 and done is not None:
                plan.append(("mix", "inv", done, 0))
            if s < 2 and u <= A_UNITS:
                misc.append(("m", "v", u, s))
            if s == 2 and done is not None:
                plan.append(("mix", "y", done))
            if s == 2 and u:
                misc.append(("m", "o", u - 1, 0))
            if s == 3 and u:
                misc.append(("m", "o", u - 1, 1))
            if s == 2 and u in (3, 6):
                plan.append(("mix", "ln", u // 3 - 1))
            start = {3: 0, 4: 1, 6: 2, 7: 3}.get(u)
            if s == 3 and start is not None:
                misc += [("m", "lse", start // 2, start % 2, g) for g in range(3)]
            if misc:
                plan.append(misc.pop(0))
            if 0 <= c - T_LAG < CHUNKS:
                plan.append(("t", c - T_LAG))
            if misc:
                plan.append(misc.pop(0))
            if 0 <= c - PV_LAG < CHUNKS:
                plan.append(("pv", c - PV_LAG))
            if misc:
                plan.append(misc.pop(0))
            if n_jobs == 2:
                job()
            plan += misc
            refill()
            if c < CHUNKS:
                plan.append(("exp", c))
            if s == 3 and start is not None:
                plan.append(("mix", "exp", start))
            if s == 1 and done is not None:
                plan.append(("mix", "inv", done, 1))
    assert next(jobs, None) is None
    return plan


PLAN = attention_plan()
M_EVENTS = [e for e in PLAN if e[0] == "m"]
M_INDEX = {e: n for n, e in enumerate(M_EVENTS)}
BIAS_BANK = (2, 5, 6, 7)


def misc_bank(m):
    return BIAS_BANK[m % 4] if M_EVENTS[m][1] == "bias" else 7


NORM_BANK = ((4, 5), (3, 4), (3, 4), (3, 4))
LATE = 2
DVE_HALF_0, DVE_HALF_1 = 4, 5
RESULT_ORDER = [(0, k) for k in (0, 1, 4, 2, 3, 5, 6, 7)] + [(1, k) for k in (0, 1, 5, 2, 3, 6, 4, 7)]


def build(nc, xT, stream, gains, b_in, sinks, rel_bias, onehot, bias_rows, h_spill, outT):
    f32, f32r = mybir.dt.float32, mybir.dt.float32r
    ALU = mybir.AluOpType
    ACT = mybir.ActivationFunctionType

    BASE = 4224
    K = 1024
    names = iter(range(1000))

    def place(name, shape, offset, dtype=f32):
        return nc.alloc_sbuf_tensor_at(f"{name}_{next(names)}", shape, dtype, offset=BASE + offset)

    ident = place("ident", [P, P], 0)
    ones = place("ones", [P, P], 512)
    bias_in = place("bias_in", [P, BIN_TILES], 1024)
    bias_q = place("bias_q", [P, BIN_TILES], 1184)
    gain = place("gain", [P, 4, KT], 1344)
    sink = place("sink", [P, B_HEADS], 1472)
    eps = place("eps", [P, 1], 1504)
    gate_bias = place("gate_bias", [P, 4], 1536)
    R = 1568

    def at(k):
        return R + int(k * K)

    h = place("h", [P, KT, SEQ], at(0))
    xh = place("xh", [P, KT, SEQ], at(32), f32r)
    xl = place("xl", [P, KT, SEQ], at(64), f32r)
    hg = place("hg", [P, KT, SEQ], at(32))
    wh = [place(f"wh{s}", [P, UNIT], at(96 + 8 * s), f32r) for s in range(FFN_UNITS)]
    wl = [place(f"wl{s}", [P, UNIT], at(100 + 8 * s), f32r) for s in range(FFN_UNITS)]
    raw = [place(f"raw{s}", [P, UNIT], at(144 + 4 * s)) for s in range(2)]
    gh = place("gh", [P, 2, SEQ], at(152), f32r)
    gl = place("gl", [P, 2, SEQ], at(160), f32r)
    tmp = [place(f"tmp{s}", [P, HALF], at(168 + 2 * s)) for s in range(4)]
    rows = place("rows", [B_HEADS, 4, VEC], at(176))
    skew = place("skew", [P, HEADS, 2 * P], at(176))
    flip = place("flip", [P, P], at(196))
    tab = place("tab", [N_BUCKETS + 1, HEADS], at(197))
    hot = place("hot", [N_BUCKETS + 1, 4, VEC], at(198))
    rstd = place("rstd", [P, SEQ], at(206))
    acc = [place(f"acc{s}", [P, HALF], at(210 + 2 * s)) for s in range(2)]
    sq = [place(f"sq{s}", [P, HALF], at(214 + 2 * s)) for s in range(2)]
    qs = [place("q0", [P, SEQ], at(0)), place("q1", [P, SEQ], at(4))]
    ks = [place("k0", [P, SEQ], at(8)), place("k1", [P, SEQ], at(190))]
    vs = [place("v0", [P, QT, P], at(12)), place("v1", [P, QT, P], at(194))]
    vt = place("vt", [P, SEQ], at(16))
    ob = place("ob", [P, QT, P], at(20))
    sp = [place(f"sp{s}", [P, 4, 2 * P], at((24, 28, 140)[s])) for s in range(3)]
    bias_B = place("bias_B", [P, B_HEADS, 2 * P], at(152))
    pt = [place(f"pt{s}", [P, 4, 2 * P], at(160 + 4 * s)) for s in range(2)]
    bias_2 = place("bias_2", [P, A_SLOTS, P], at(168))
    negm = place("negm", [P, 4 * CHUNKS], at(170))
    den = place("den", [P, 4 * CHUNKS], at(170) + 640)
    sexp = place("sexp", [P, 4 * 4 * B_UNITS], at(170) + 1280)
    ln_den = place("ln_den", [P, 3, 2, QT], at(170) + 1536)
    rmax = place("rmax", [P, 2, 4], at(170) + 1728)
    rden = place("rden", [P, 2, 4], at(170) + 1760)
    bias_A = place("bias_A", [P, 2 * A_SLOTS, 2 * P], at(198))
    Y = [174 + 4 * n for n in range(8)] + [128 + 4 * n for n in range(3)]
    yah = [place(f"yah{p}", [P, SEQ], at(Y[2 * p]), f32r) for p in range(2)]
    yal = [place(f"yal{p}", [P, SEQ], at(Y[2 * p + 1]), f32r) for p in range(2)]
    og = [place(f"og{g}", [P, SEQ], at((Y[8], Y[9], Y[10], 210)[g])) for g in range(4)]
    scaled = [place(f"scaled{s}", [P, HALF], at(214 + 2 * s)) for s in range(2)]
    YB = (6, 10, 8, 4)
    ybh = [place(f"ybh{i}", [P, SEQ], at(Y[YB[i]]), f32r) for i in range(B_UNITS)]
    ybl = [place(f"ybl{i}", [P, SEQ], at(210 if i == 1 else Y[YB[i] + 1]), f32r) for i in range(B_UNITS)]
    wide_0 = place("wide_0", [P, 4, 2, HD], at(172))
    wide_1 = [place(f"wide_1{p}", [P, 4, 2, HD], at(Y[(2, 4)[p]] + 6)) for p in range(2)]
    mix = [[place(f"mix{p}{n}", [P, HALF], at(Y[(2, 4)[p]] + 2 * n)) for n in range(4)] for p in range(2)]

    ctx = ExitStack()
    with ctx:
        bank = [ctx.enter_context(nc.psum_tensor(f"bank{n}", [P, HALF], f32)) for n in range(8)]

        def sem(name):
            return ctx.enter_context(nc.semaphore(name))

        x_in = [sem(f"x_in{n}") for n in range(5)]
        gain_in = sem("gain_in")
        const_in = sem("const_in")
        tab_in = sem("tab_in")
        raw_in = [sem("raw_in0"), sem("raw_in1")]
        rows_out = sem("rows_out")
        skew_in = sem("skew_in")
        spilled = sem("spilled")
        h_back = sem("h_back")
        stored = sem("stored")
        made = sem("made")
        bias_scaled = sem("bias_scaled")
        vec_done = sem("vec_done")
        vec_out = sem("vec_out")
        w_high = sem("w_high")
        w_low = sem("w_low")
        sq_done = sem("sq_done")
        sq_sum = sem("sq_sum")
        ssq = sem("ssq")
        root = sem("root")
        rstd_done = sem("rstd_done")
        x_high = sem("x_high")
        x_low = sem("x_low")
        x_gain = sem("x_gain")
        x_out = sem("x_out")
        x_out_p = sem("x_out_p")
        gu_done = sem("gu_done")
        gu_out = sem("gu_out")
        silu_done = sem("silu_done")
        prod_done = sem("prod_done")
        g_high = sem("g_high")
        g_low = sem("g_low")
        down_done = sem("down_done")
        down_added = sem("down_added")
        job_done = sem("job_done")
        job_scaled = sem("job_scaled")
        job_out = sem("job_out")
        qk_done = sem("qk_done")
        max_done = sem("max_done")
        negm_done = sem("negm_done")
        exp_done = sem("exp_done")
        t_done = sem("t_done")
        t_out = [sem("t_out0"), sem("t_out1")]
        pv_done = sem("pv_done")
        den_done = sem("den_done")
        pv_out = sem("pv_out")
        m_done = sem("m_done")
        m_out = sem("m_out")
        mask_set = sem("mask_set")
        yb_high = sem("yb_high")
        ln_done = sem("ln_done")
        wide_done = sem("wide_done")
        mix_top = sem("mix_top")
        mix_diff = sem("mix_diff")
        mix_exp = sem("mix_exp")
        mix_sum = sem("mix_sum")
        mix_inv = sem("mix_inv")
        mix_part = sem("mix_part")
        mix_y = sem("mix_y")
        ya_high = sem("ya_high")
        y_low = sem("y_low")
        part_done = sem("part_done")
        gate_bias_set = sem("gate_bias_set")
        sig_done = sem("sig_done")
        mul_done = sem("mul_done")
        m_high = sem("m_high")
        m_low = sem("m_low")

        block = ctx.enter_context(nc.Block())

        def fold(buf, g, hf):
            if g == 0:
                return buf[:, hf * HALF:(hf + 1) * HALF]
            d = DILATIONS[g]
            n = HALF // d
            return buf[:, :].rearrange("p (r b q) -> p q r b", r=d, b=2)[:, 0:n, :, hf]

        def unfold(buf, g, hf):
            if g == 0:
                return buf[:, hf * HALF:(hf + 1) * HALF]
            if g == 1:
                return buf[:, :].rearrange("p (b q r) -> p r b q", b=2, r=4)[:, 2 * hf:2 * hf + 2]
            return buf[:, :].rearrange("p (j r) -> p r j", r=16)[:, 8 * hf:8 * hf + 8]

        def has_previous(u, tile):
            kind, _, g = unit_of(u)
            return tile > 0 if g == 0 else g == 1 and tile % 2 == 1

        def transposed(c, b):
            _, _, g = unit_of(c // 4)
            src = bank[4 + b][:].rearrange("p (i k) -> p i k", i=2)
            dst = pt[c % 2][:, 2 * b:2 * b + 2, :]
            if g == 2:
                return dst[:, :, P:], src[:, :, P:]
            if not has_previous(c // 4, 4 * (c % 2) + 2 * b):
                return dst.rearrange("p i k -> p (i k)")[:, P:], bank[4 + b][:, P:]
            return dst, src

        DOWN_MERGE = 16 * FFN_STEPS
        DOWN_FFN2 = DOWN_MERGE + 16 * MERGE_STEPS

        @block.sync
        def _(sp_):
            x_t = xT.rearrange("(k p) t -> p k t", p=P)
            sp_.dma_start(raw[0][:], stream[0]).then_inc(raw_in[0], 16)
            for n in range(4):
                sp_.dma_start(h[:, 2 * n:2 * n + 2, 0:HALF], x_t[:, 2 * n:2 * n + 2, 0:HALF]).then_inc(x_in[n], 16)
                if n == 1:
                    sp_.dma_start(raw[1][:], stream[1]).then_inc(raw_in[1], 16)
            sp_.dma_start(h[:, :, HALF:], x_t[:, :, HALF:]).then_inc(x_in[4], 16)
            with sp_.Fori(1, N_UNITS // 2) as n:
                for s in range(2):
                    sp_.wait_ge(w_low, 2 * n - 1 + s)
                    sp_.dma_start(raw[s][:], stream[2 * n + s]).then_inc(raw_in[s], 16)
            for hf, k in RESULT_ORDER:
                cols = slice(hf * HALF, (hf + 1) * HALF)
                by_dve = (DVE_HALF_0, DVE_HALF_1)[hf]
                if k < by_dve:
                    sp_.wait_ge(x_out, (DVE_HALF_0 if hf else 0) + k + 1)
                else:
                    sp_.wait_ge(x_out_p, (KT - DVE_HALF_0 if hf else 0) + k - by_dve + 1)
                sp_.dma_start(outT[k * P:(k + 1) * P, cols], hg[:, k, cols]).then_inc(stored, 16)
            sp_.wait_ge(stored, 16 * 16)

        @block.gpsimd
        def _(pool):
            nc.gpsimd.memset(eps[:], EPS).then_inc(made, 1)
            pool.dma_start(tab[0:N_BUCKETS, :], rel_bias).then_inc(tab_in, 16)
            pool.dma_start(hot[:], onehot).then_inc(tab_in, 16)
            pool.dma_start(bias_in[:], b_in).then_inc(const_in, 16)
            pool.dma_start(sink[:], sinks.partition_broadcast(P)).then_inc(const_in, 16)
            nc.gpsimd.memset(ones[:], 1.0 / D_MODEL).then_inc(made, 1)
            nc.gpsimd.memset(ident[:], 0.0).then_inc(made, 1)
            nc.gpsimd.memset(flip[:], 0.0).then_inc(made, 1)
            pool.wait_ge(made, 4)
            nc.gpsimd.memset(tab[N_BUCKETS:, :], NEG).then_inc(made, 1)
            pool.wait_ge(made, 5)
            nc.gpsimd.affine_select(out=ident[:], in_=ident[:], compare_op=ALU.not_equal, fill=1.0, base=0,
                                    pattern=[[-1, P]], channel_multiplier=1).then_inc(made, 1)
            nc.gpsimd.affine_select(out=flip[:], in_=flip[:], compare_op=ALU.not_equal, fill=1.0,
                                    base=1 - P, pattern=[[1, P]], channel_multiplier=1).then_inc(made, 1)

            def add_squares(norm, hf):
                base = (KT - 1) * (2 * norm + hf)
                for k in range(1, KT - LATE if (norm, hf) == (3, 1) else KT):
                    pool.wait_ge(sq_done, 16 * norm + 8 * hf + k + 1)
                    if k > 1:
                        pool.wait_ge(sq_sum, base + k - 1)
                    nc.gpsimd.tensor_tensor(acc[hf][:], (sq[0] if k == 1 else acc[hf])[:], sq[k % 2][:], ALU.add).then_inc(sq_sum, 1)

            add_squares(0, 0)
            add_squares(0, 1)
            pool.wait_ge(vec_out, 4)
            for v, (first, n) in enumerate(((0, 4), (4, 4), (8, 4), (12, 8))):
                pool.dma_start(bias_rows[first:first + n, :], rows[0:n, v, :]).then_inc(rows_out, 16)
            pool.wait_ge(rows_out, 64)
            pool.dma_start(skew[:], bass.AP(tensor=bias_rows.tensor, offset=bias_rows.offset,
                                            ap=[[1, P], [VEC, HEADS], [1, 2 * P]])).then_inc(skew_in, 16)
            add_squares(1, 0)
            add_squares(1, 1)
            for n in range(4):
                pair, hf = n // 2, n % 2
                w, total = mix[pair][0:3], mix[pair][3]
                outs = [og[(3 * pair + g) % 4][:, hf * HALF:(hf + 1) * HALF] for g in range(3)]
                pool.wait_ge(ln_done, pair + 1)
                for b, (g, tiles) in enumerate(((0, slice(4 * hf, 4 * hf + 4)), (1, slice(hf, QT, 2)),
                                                (2, slice(0, 4)), (2, slice(4, QT)))):
                    if b >= 2 or n:
                        pool.wait_ge(m_done, M_INDEX[("m", "lse", pair, hf, b - 2) if b >= 2 else ("m", "lse", (n - 1) // 2, (n - 1) % 2, 2)] + 1)
                    if b == 1 and n:
                        pool.wait_ge(y_low, n)
                    if b == 1 and n == 2:
                        pool.wait_ge(pv_done, 4 * A_UNITS)
                    first = 48 * pair + 16 * g
                    minus_max = negm[:, first:first + 16].rearrange("p (a t) -> p t a", a=2)[:, tiles, :]
                    ln = ln_den[:, g, :, :].rearrange("p a t -> p t a")[:, tiles, :]
                    nc.gpsimd.tensor_tensor((wide_0 if b % 2 == 0 else wide_1[pair])[:], ln.unsqueeze(3).to_broadcast([P, 4, 2, HD]),
                                            minus_max.unsqueeze(3).to_broadcast([P, 4, 2, HD]), ALU.subtract).then_inc(wide_done, 1)
                pool.wait_ge(mix_top, 2 * n + 2)
                for g in range(3):
                    nc.gpsimd.tensor_tensor(w[g][:], w[g][:], total[:], ALU.subtract).then_inc(mix_diff, 1)
                pool.wait_ge(mix_exp, 3 * n + 2)
                pool.wait_ge(mix_diff, 3 * n + 3)
                nc.gpsimd.tensor_tensor(total[:], w[0][:], w[1][:], ALU.add).then_inc(mix_sum, 1)
                pool.wait_ge(mix_exp, 3 * n + 3)
                pool.wait_ge(mix_sum, 2 * n + 1)
                nc.gpsimd.tensor_tensor(total[:], total[:], w[2][:], ALU.add).then_inc(mix_sum, 1)
                pool.wait_ge(m_out, M_INDEX[("m", "o", 3 * pair + 2, 1)] + 1)
                for g in range(3):
                    nc.gpsimd.tensor_tensor(outs[g], outs[g], w[g][:], ALU.mult).then_inc(mix_part, 1)
                pool.wait_ge(mix_part, 5 * n + 2)
                nc.gpsimd.tensor_tensor(outs[0], outs[0], outs[1], ALU.add).then_inc(mix_part, 1)
                pool.wait_ge(mix_part, 5 * n + 4)
                nc.gpsimd.tensor_tensor(outs[0], outs[0], outs[2], ALU.add).then_inc(mix_part, 1)
                pool.wait_ge(mix_part, 5 * n + 5)
                pool.wait_ge(mix_inv, 2 * n + 2)
                nc.gpsimd.tensor_tensor(total[:], outs[0], total[:], ALU.mult).then_inc(mix_y, 1)
            for norm in (2, 3):
                for hf in range(2):
                    add_squares(norm, hf)
            for hf in range(2):
                cols = slice(hf * HALF, (hf + 1) * HALF)
                pool.wait_ge(rstd_done, 7 + hf)
                for k in range((DVE_HALF_0, DVE_HALF_1)[hf], KT):
                    pool.wait_ge(x_gain, KT * hf + k + 1)
                    nc.gpsimd.tensor_tensor(hg[:, k, cols], hg[:, k, cols], rstd[:, cols], ALU.mult).then_inc(x_out_p, 1)

        @block.scalar
        def _(act):
            act.dma_start(gain[:], gains).then_inc(gain_in, 16)
            act.wait_ge(made, 1)
            nc.scalar.activation(gate_bias[:, 0:1], eps[:], ACT.Copy)

            def split_high(u, parity, slot, free=None):
                act.wait_ge(raw_in[parity], 8 * (u - parity) + 16)
                if free:
                    act.wait_ge(*free)
                nc.scalar.activation(wh[slot][:], raw[parity][:], ACT.Copy).then_inc(w_high, 1)

            def high(norm, hf, k):
                cols = slice(hf * HALF, (hf + 1) * HALF)
                if norm == 0:
                    act.wait_ge(x_in[k // 2 if hf == 0 else 4], 16)
                else:
                    first = (0, DOWN_MERGE, DOWN_FFN2)[norm] - 16
                    act.wait_ge(down_added, first + 8 * hf + k + 1)
                nc.scalar.activation(xh[:, k, cols], h[:, k, cols], ACT.Copy, scale=gain[:, norm, k:k + 1]).then_inc(x_high, 1)

            def square(norm, hf, k):
                cols = slice(hf * HALF, (hf + 1) * HALF)
                base = (KT - 1) * (2 * norm + hf)
                if norm == 3:
                    act.wait_ge(down_added, DOWN_FFN2 + 16 * FFN_STEPS - 16 + 8 * hf + k + 1)
                free = base - 1 + k if k < 2 else base + max(1, k - 2)
                if free > 0:
                    act.wait_ge(sq_sum, free)
                nc.scalar.activation(sq[k % 2][:], h[:, k, cols], ACT.Square).then_inc(sq_done, 1)
                if norm == 1:
                    act.dma_start(h_spill[:, k, cols], h[:, k, cols]).then_inc(spilled, 16)
                if norm == 3:
                    nc.scalar.activation(hg[:, k, cols], h[:, k, cols], ACT.Copy, scale=gain[:, 3, k:k + 1]).then_inc(x_gain, 1)

            def root_of(norm, hf):
                act.wait_ge(made, 1)
                act.wait_ge(ssq, 2 * norm + hf + 1)
                nc.scalar.activation(rstd[:, hf * HALF:(hf + 1) * HALF], bank[NORM_BANK[norm][hf]][:], ACT.Sqrt,
                                     bias=eps[:, 0:1]).then_inc(root, 1)

            def ffn_step(i, f, last=False):
                step = i + FFN_STEPS * f
                unit = FFN_UNITS * i + (FFN2_0 if f else 0)
                first_step = isinstance(i, int) and i == 0
                fresh = first_step and not f
                for t in range(4):
                    tile, hf = t % 2, t // 2
                    if first_step and t == (1 if f else 2):
                        root_of(2 * f, 1)
                    act.wait_ge(gu_out, 8 * step + 2 * t + 1)
                    nc.scalar.activation(tmp[t % 2][:], tmp[t % 2][:], ACT.Silu).then_inc(silu_done, 1)
                    if t < 2:
                        before = None if fresh else (down_done, 16 * step + (DOWN_FFN2 - 16 * FFN_STEPS if f else 0))
                        split_high(unit + 4 + t, t % 2, 4 + t, before)
                    if first_step and not f and t == 0:
                        for k in range(4, KT):
                            square(0, 1, k)
                    act.wait_ge(prod_done, 4 * step + t + 1)
                    nc.scalar.activation(gh[:, tile, hf * HALF:(hf + 1) * HALF], tmp[2 + t % 2][:], ACT.Copy).then_inc(g_high, 1)
                for j in range(4):
                    if last and f:
                        break
                    if last and j == 2:
                        for d in range(16):
                            high(1, d // 8, d % 8)
                            square(1, d // 8, d % 8)
                    split_high(unit + FFN_UNITS + j, j % 2, j, (gu_done, 4 * step + 3 + j // 2))
                if last and f:
                    for d in range(16):
                        square(3, d // 8, d % 8)
                        if d == 13:
                            root_of(3, 0)
                    root_of(3, 1)
                elif last:
                    root_of(1, 0)

            split_high(0, 0, 0)
            act.wait_ge(gain_in, 16)
            for k in range(KT):
                high(0, 0, k)
                if k == 3:
                    split_high(1, 1, 1)
            for k in range(KT):
                square(0, 0, k)
                if k % 4 == 3:
                    split_high(2 + k // 4, k // 4, 2 + k // 4)
            for k in range(KT):
                high(0, 1, k)
                if k == 2:
                    root_of(0, 0)
            for k in range(4):
                square(0, 1, k)
            act.wait_ge(const_in, 32)
            nc.scalar.activation(bias_q[:], bias_in[:], ACT.Copy, scale=HD ** -0.5).then_inc(bias_scaled, 1)
            ffn_step(0, 0)
            with act.Fori(1, FFN_STEPS - 1) as i:
                ffn_step(i, 0)
            ffn_step(FFN_STEPS - 1, 0, last=True)

            act.wait_ge(bias_scaled, 1)
            tiles = proj_tiles()
            for e in PLAN:
                if e[0] == "ssq":
                    root_of(1, 1)
                elif e[0] == "job":
                    n, hf = JOBS[e[1]]
                    role, u = tiles[n]
                    _, _, g = unit_of(u)
                    last_qk = {"q": 8 * (u - 1), "k": 8 * (u - 1)}.get(role)
                    act.wait_ge(job_scaled, e[1] + 1)
                    if e[1] == 0:
                        act.wait_ge(spilled, 16 * 16)
                    if hf == 0 and u >= 2 and role != "v":
                        act.wait_ge(qk_done, last_qk)
                    if hf == 0 and role == "v" and u:
                        act.wait_ge(m_done, M_INDEX[("m", "v", u - 1, 1)] + 1)
                    dst = {"q": qs[u % 2], "k": ks[u % 2], "v": vt}[role]
                    src = scaled[e[1] % 2][:] if g == 0 else scaled[e[1] % 2][:].rearrange("p (q r) -> p q r", r=DILATIONS[g])
                    nc.scalar.activation(fold(dst, g, hf), src, ACT.Identity, scale=HD ** -0.5 if role == "q" else 1.0,
                                         bias=(bias_q if role == "q" else bias_in)[:, n:n + 1]).then_inc(job_out, 1)
                elif e[0] == "w":
                    split_high(PROJ_0 + e[1] + RING, e[1] % 2, e[1] % RING, (job_done, JOB_INDEX[(e[1], 1)] + 1))
                elif e[0] == "exp":
                    c = e[1]
                    u, a, j = c // 4, c // 2 % 2, c % 2
                    act.wait_ge(negm_done, c + 1)
                    for i in range(4):
                        lo = 0 if has_previous(u, 4 * j + i) else P
                        last = nc.scalar.activation(sp[c % 3][:, i, lo:], sp[c % 3][:, i, lo:], ACT.Exp,
                                                    bias=negm[:, 4 * c + i:4 * c + i + 1],
                                                    accum_out=den[:, 4 * c + i:4 * c + i + 1])
                    if u >= A_UNITS:
                        head = u - A_UNITS + B_UNITS * a
                        s = 4 * (c - 4 * A_UNITS)
                        last = nc.scalar.activation(sexp[:, s:s + 4], negm[:, 4 * c:4 * c + 4], ACT.Exp, bias=sink[:, head:head + 1])
                    last.then_inc(exp_done, 1)
                elif e[0] == "t":
                    c = e[1]
                    act.wait_ge(t_done, 2 * c + 2)
                    dst, src = transposed(c, 1)
                    nc.scalar.activation(dst, src, ACT.Copy).then_inc(t_out[1], 1)
                elif e[0] == "mix" and e[1] == "exp":
                    for g in range(3):
                        act.wait_ge(mix_diff, 3 * e[2] + g + 1)
                        w = mix[e[2] // 2][g]
                        nc.scalar.activation(w[:], w[:], ACT.Exp).then_inc(mix_exp, 1)
                elif e[0] == "mix" and e[1] == "y":
                    pair, hf = e[2] // 2, e[2] % 2
                    act.wait_ge(mix_y, e[2] + 1)
                    nc.scalar.activation(yah[pair][:, hf * HALF:(hf + 1) * HALF], mix[pair][3][:], ACT.Copy).then_inc(ya_high, 1)
                elif e[:2] == ("m", "o") and e[2] >= A_UNITS:
                    i, hf = e[2] - A_UNITS, e[3]
                    act.wait_ge(m_done, M_INDEX[e] + 1)
                    if i:
                        act.wait_ge(y_low, 4)
                    nc.scalar.activation(ybh[i][:, hf * HALF:(hf + 1) * HALF], bank[7][:], ACT.Copy).then_inc(yb_high, 1)
                elif e[:2] == ("mix", "ln"):
                    pair = e[2]
                    if pair:
                        act.wait_ge(wide_done, 8)
                    nc.scalar.activation(ln_den[:].rearrange("p g a t -> p (g a t)"), den[:, 48 * pair:48 * pair + 48], ACT.Ln).then_inc(ln_done, 1)

            def merge_step(i, last=False):
                unit = MERGE_0 + MERGE_UNITS * i
                nc.scalar.activation(gate_bias[:], bias_in[:, bass.ds(PROJ + 4 * i, 4)], ACT.Copy).then_inc(gate_bias_set, 1)
                act.wait_ge(gate_bias_set, i + 1)
                for t in range(4):
                    tile, hf = t // 2, t % 2
                    job = 4 * i + t
                    for gate in range(2):
                        act.wait_ge(mul_done, 5 * job + 2 * gate + 1)
                        nc.scalar.activation(tmp[gate][:], tmp[gate][:], ACT.Sigmoid,
                                             bias=gate_bias[:, 2 * tile + gate:2 * tile + gate + 1]).then_inc(sig_done, 1)
                        if hf:
                            j = 3 * tile + gate + RING
                            split_high(unit + j, j % 2, j % RING, (part_done, 4 * job + 2 * gate + 1))
                    act.wait_ge(mul_done, 5 * job + 5)
                    nc.scalar.activation(gh[:, tile, hf * HALF:(hf + 1) * HALF], tmp[2][:], ACT.Copy).then_inc(m_high, 1)
                    if hf:
                        j = 3 * tile + 2 + RING
                        split_high(unit + j, j % 2, j % RING, (part_done, 4 * job + 4))
                if last:
                    for d in range(16):
                        high(2, d // 8, d % 8)
                        square(2, d // 8, d % 8)
                for j in range(2):
                    split_high(unit + 10 + j, j % 2, 2 + j, (down_done, DOWN_MERGE + 16 * i + 16))

            act.wait_ge(m_out, len(M_EVENTS))
            act.wait_ge(spilled, 16 * 16)
            act.dma_start(h[:], h_spill[:, :, :]).then_inc(h_back, 16)
            with act.Fori(0, MERGE_STEPS - 1) as i:
                merge_step(i)
            merge_step(MERGE_STEPS - 1, last=True)
            root_of(2, 0)
            ffn_step(0, 1)
            with act.Fori(1, FFN_STEPS - 1) as i:
                ffn_step(i, 1)
            ffn_step(FFN_STEPS - 1, 1, last=True)

        @block.vector
        def _(dve):
            def split_low(u, parity, slot):
                dve.wait_ge(w_high, u + 1)
                nc.vector.tensor_tensor(wl[slot][:], raw[parity][:], wh[slot][:], ALU.subtract).then_inc(w_low, 1)

            def low(norm, hf, k):
                cols = slice(hf * HALF, (hf + 1) * HALF)
                dve.wait_ge(x_high, 16 * norm + 8 * hf + k + 1)
                nc.vector.scalar_tensor_tensor(out=xl[:, k, cols], in0=h[:, k, cols], scalar=gain[:, norm, k:k + 1],
                                               in1=xh[:, k, cols], op0=ALU.mult, op1=ALU.subtract).then_inc(x_low, 1)

            def invert_part(norm, hf, part, of):
                cols = slice(hf * HALF + part * HALF // of, hf * HALF + (part + 1) * HALF // of)
                dve.wait_ge(root, 2 * norm + hf + 1)
                last = nc.vector.reciprocal(rstd[:, cols], rstd[:, cols])
                if part == of - 1:
                    last.then_inc(rstd_done, 1)

            def invert(norm, hf):
                invert_part(norm, hf, 0, 1)
                dve.wait_ge(rstd_done, 2 * norm + hf + 1)

            def result(hf, k):
                cols = slice(hf * HALF, (hf + 1) * HALF)
                dve.wait_ge(x_gain, KT * hf + k + 1)
                nc.vector.tensor_tensor(hg[:, k, cols], hg[:, k, cols], rstd[:, cols], ALU.mult).then_inc(x_out, 1)

            def ffn_step(i, f, last=False):
                step = i + FFN_STEPS * f
                unit = FFN_UNITS * i + (FFN2_0 if f else 0)
                first_step = isinstance(i, int) and i == 0
                for t in range(4):
                    tile, hf = t % 2, t // 2
                    cols = slice(hf * HALF, (hf + 1) * HALF)
                    dve.wait_ge(gu_done, 4 * step + t + 1)
                    if not (first_step and not f and t < 2):
                        dve.wait_ge(g_low, 4 * step + t - 1)
                    for part in range(2):
                        nc.vector.tensor_tensor(tmp[2 * part + t % 2][:], bank[2 * (t % 2) + part][:], rstd[:, cols], ALU.mult).then_inc(gu_out, 1)
                    if first_step and not f and t == 0:
                        for k in range(2, KT):
                            low(0, 1, k)
                    if t < 2:
                        split_low(unit + 4 + t, t % 2, 4 + t)
                    dve.wait_ge(gu_out, 8 * step + 2 * t + 2)
                    dve.wait_ge(silu_done, 4 * step + t + 1)
                    nc.vector.tensor_tensor(tmp[2 + t % 2][:], tmp[t % 2][:], tmp[2 + t % 2][:], ALU.mult).then_inc(prod_done, 1)
                    dve.wait_ge(g_high, 4 * step + t + 1)
                    nc.vector.tensor_tensor(gl[:, tile, cols], tmp[2 + t % 2][:], gh[:, tile, cols], ALU.subtract).then_inc(g_low, 1)
                    if first_step and t == (0 if f else 1):
                        invert(2 * f, 1)
                first = 16 * step + (DOWN_FFN2 - 16 * FFN_STEPS if f else 0)
                for d in range(16):
                    hf, k = d // 8, d % 8
                    cols = slice(hf * HALF, (hf + 1) * HALF)
                    dve.wait_ge(down_done, first + d + 1)
                    nc.vector.scalar_tensor_tensor(out=h[:, k, cols], in0=bank[4 + d % 4][:], scalar=0.5, in1=h[:, k, cols],
                                                   op0=ALU.mult, op1=ALU.add).then_inc(down_added, 1)
                    if last and not f:
                        if d in (1, 3):
                            split_low(unit + FFN_UNITS + d // 2, d // 2, d // 2)
                        if d:
                            low(1, (d - 1) // 8, (d - 1) % 8)
                    elif last and d >= 13:
                        invert_part(3, 0, d - 13, 4)
                    elif d % 4 == 1 and not last:
                        split_low(unit + FFN_UNITS + d // 4, d // 4 % 2, d // 4)
                if last and not f:
                    low(1, 1, KT - 1)
                    for j in range(2, 4):
                        split_low(unit + FFN_UNITS + j, j % 2, j)
                    invert(1, 0)
                elif last:
                    invert_part(3, 0, 3, 4)
                    dve.wait_ge(rstd_done, 7)
                    for k in range(DVE_HALF_0):
                        result(0, k)
                    invert(3, 1)
                    for k in range(DVE_HALF_1):
                        result(1, k)

            dve.wait_ge(gain_in, 16)
            split_low(0, 0, 0)
            for k in range(4):
                low(0, 0, k)
            split_low(1, 1, 1)
            for k in range(4, KT):
                low(0, 0, k)
            for j in range(2, 4):
                split_low(j, j % 2, j)
            for v, n in enumerate((4, 4, 4, 8)):
                dve.wait_ge(vec_done, v + 1)
                nc.vector.tensor_copy(rows[0:n, v, :], bank[4 + v][0:n, 0:VEC]).then_inc(vec_out, 1)
            for k in range(2):
                low(0, 1, k)
            invert(0, 0)
            ffn_step(0, 0)
            with dve.Fori(1, FFN_STEPS - 1) as i:
                ffn_step(i, 0)
            ffn_step(FFN_STEPS - 1, 0, last=True)

            for e in PLAN:
                if e[0] == "exp":
                    continue
                if e[0] == "ssq":
                    invert(1, 1)
                elif e[0] == "job":
                    n, hf = JOBS[e[1]]
                    dve.wait_ge(job_done, e[1] + 1)
                    if e[1] == 0:
                        dve.wait_ge(sq_sum, 4 * (KT - 1))
                    if e[1] >= 2:
                        dve.wait_ge(job_out, e[1] - 1)
                    nc.vector.tensor_tensor(scaled[e[1] % 2][:], bank[e[1] % 2][:], rstd[:, hf * HALF:(hf + 1) * HALF],
                                            ALU.mult).then_inc(job_scaled, 1)
                elif e[0] == "w":
                    split_low(PROJ_0 + e[1] + RING, e[1] % 2, e[1] % RING)
                elif e[0] == "qk":
                    c = e[1]
                    u, a, j = c // 4, c // 2 % 2, c % 2
                    kind, pair, g = unit_of(u)
                    for i in range(4):
                        lo = 0 if has_previous(u, 4 * j + i) else P
                        if i % 2 == 0:
                            dve.wait_ge(qk_done, 2 * c + i // 2 + 1)
                        head = pair + B_UNITS * a if kind == "B" else A_SLOTS * g + 2 * pair + a
                        bias = bias_B[:, head, lo:] if kind == "B" else bias_A[:, head, lo:] if g < 2 else bias_2[:, head - 2 * A_SLOTS, :]
                        nc.vector.tensor_tensor_reduce(out=sp[c % 3][:, i, lo:], in0=bank[2 + i // 2][:, i % 2 * 2 * P + lo:(i % 2 + 1) * 2 * P],
                                                       in1=bias, scale=1.0, scalar=3 * NEG, op0=ALU.add, op1=ALU.max,
                                                       accum_out=rmax[:, c % 2, i:i + 1]).then_inc(max_done, 1)
                    dve.wait_ge(max_done, 4 * c + 4)
                    floor = sink[:, head:head + 1] if kind == "B" else 3 * NEG
                    nc.vector.tensor_scalar(negm[:, 4 * c:4 * c + 4], rmax[:, c % 2, :], floor, -1.0, ALU.max, ALU.mult).then_inc(negm_done, 1)
                elif e[0] == "t":
                    c = e[1]
                    dve.wait_ge(t_done, 2 * c + 1)
                    dst, src = transposed(c, 0)
                    nc.vector.tensor_copy(dst, src).then_inc(t_out[0], 1)
                elif e[0] == "mix":
                    n = e[2]
                    pair, hf = n // 2, n % 2
                    if e[1] == "inv":
                        dve.wait_ge(mix_sum, 2 * n + 2)
                        part = mix[pair][3][:, e[3] * HALF // 2:(e[3] + 1) * HALF // 2]
                        nc.vector.reciprocal(part, part).then_inc(mix_inv, 1)
                    elif e[1] == "y":
                        cols = slice(hf * HALF, (hf + 1) * HALF)
                        dve.wait_ge(ya_high, n + 1)
                        nc.vector.tensor_tensor(yal[pair][:, cols], mix[pair][3][:], yah[pair][:, cols], ALU.subtract).then_inc(y_low, 1)
                elif e[0] == "pv":
                    c = e[1]
                    u, a, j = c // 4, c // 2 % 2, c % 2
                    total = den[:, 4 * c:4 * c + 4]
                    dve.wait_ge(pv_done, c + 1)
                    if u >= A_UNITS:
                        s = 4 * (c - 4 * A_UNITS)
                        nc.vector.tensor_tensor(total, total, sexp[:, s:s + 4], ALU.add).then_inc(den_done, 1)
                        dve.wait_ge(den_done, c + c - 4 * A_UNITS + 1)
                    nc.vector.reciprocal(rden[:, c % 2, :], total).then_inc(den_done, 1)
                    dve.wait_ge(den_done, c + 1 + max(0, c - 4 * A_UNITS + 1))
                    nc.vector.tensor_tensor(ob[:, 4 * j:4 * j + 4, a * HD:(a + 1) * HD],
                                            bank[6][:, 0:4 * HD].rearrange("p (i d) -> p i d", i=4),
                                            rden[:, c % 2, :].unsqueeze(2).to_broadcast([P, 4, HD]), ALU.mult).then_inc(pv_out, 1)
                else:
                    m = M_INDEX[e]
                    dve.wait_ge(m_done, m + 1)
                    if e[1] == "bias":
                        n = e[2]
                        src = bank[misc_bank(m)][:].rearrange("p (h k) -> p h k", h=2)
                        if n < 4:
                            nc.vector.tensor_copy(bias_A[:, 2 * n:2 * n + 2, :], src).then_inc(m_out, 1)
                        elif n < 6:
                            nc.vector.tensor_copy(bias_2[:, 2 * n - 8:2 * n - 6, :], src[:, :, P:]).then_inc(m_out, 1)
                            if n == 5:
                                dve.wait_ge(m_out, m + 1)
                                nc.vector.memset(bias_2[HD:, :, 0:HD], NEG).then_inc(mask_set, 1)
                                dve.wait_ge(mask_set, 1)
                        else:
                            nc.vector.tensor_copy(bias_B[:, 2 * n - 12:2 * n - 10, :], src).then_inc(m_out, 1)
                    elif e[1] == "v":
                        u, hf = e[2], e[3]
                        nc.vector.tensor_copy(vs[u % 2][:, 4 * hf:4 * hf + 4, :], bank[7][:].rearrange("p (i d) -> p i d", i=4)).then_inc(m_out, 1)
                    elif e[1] == "o":
                        u, hf = e[2], e[3]
                        kind, i, g = unit_of(u)
                        if kind == "A":
                            dst = unfold(og[u % 4], g, hf)
                            if u >= 4:
                                dve.wait_ge(mix_y, 2)
                            src = bank[7][:]
                            if g == 1:
                                src = src.rearrange("p (r b q) -> p r b q", r=2, b=2)
                            elif g == 2:
                                src = src.rearrange("p (r j) -> p r j", r=8)
                            nc.vector.tensor_copy(dst, src).then_inc(m_out, 1)
                        else:
                            cols = slice(hf * HALF, (hf + 1) * HALF)
                            dve.wait_ge(yb_high, 2 * i + hf + 1)
                            nc.vector.tensor_tensor(ybl[i][:, cols], bank[7][:], ybh[i][:, cols], ALU.subtract).then_inc(m_out, 1)
                    elif e[1] == "lse":
                        pair, hf, g = e[2:]
                        dst, src = mix[pair][g][:], bank[7][:]
                        if g:
                            dst = dst.rearrange("p (j r) -> p r j", r=DILATIONS[g])
                            src = src.rearrange("p (r j) -> p r j", r=DILATIONS[g])
                        nc.vector.tensor_copy(dst, src).then_inc(m_out, 1)
                        if g == 2:
                            top, n = mix[pair][3], 2 * pair + hf
                            dve.wait_ge(m_out, m + 1)
                            if n:
                                dve.wait_ge(y_low, n)
                            nc.vector.tensor_tensor(top[:], mix[pair][0][:], mix[pair][1][:], ALU.max).then_inc(mix_top, 1)
                            dve.wait_ge(mix_top, 2 * n + 1)
                            nc.vector.tensor_tensor(top[:], top[:], mix[pair][2][:], ALU.max).then_inc(mix_top, 1)

            def merge_step(i, last=False):
                unit = MERGE_0 + MERGE_UNITS * i
                for t in range(4):
                    tile, hf = t // 2, t % 2
                    job = 4 * i + t
                    cols = slice(hf * HALF, (hf + 1) * HALF)
                    if not (isinstance(job, int) and job == 0):
                        dve.wait_ge(m_low, job)
                    for gate in range(2):
                        dve.wait_ge(part_done, 4 * job + 2 * gate + 1)
                        if not (isinstance(job, int) and job == 0):
                            dve.wait_ge(mul_done, 5 * job)
                        nc.vector.tensor_tensor(tmp[gate][:], bank[2 * gate][:], rstd[:, cols], ALU.mult).then_inc(mul_done, 1)
                        dve.wait_ge(sig_done, 2 * job + gate + 1)
                        dve.wait_ge(part_done, 4 * job + 2 * gate + 2)
                        nc.vector.tensor_tensor(tmp[gate][:], tmp[gate][:], bank[2 * gate + 1][:], ALU.mult).then_inc(mul_done, 1)
                        if hf:
                            j = 3 * tile + gate + RING
                            split_low(unit + j, j % 2, j % RING)
                    dve.wait_ge(mul_done, 5 * job + 4)
                    nc.vector.tensor_tensor(tmp[2][:], tmp[0][:], tmp[1][:], ALU.add).then_inc(mul_done, 1)
                    dve.wait_ge(m_high, job + 1)
                    nc.vector.tensor_tensor(gl[:, tile, cols], tmp[2][:], gh[:, tile, cols], ALU.subtract).then_inc(m_low, 1)
                    if hf:
                        j = 3 * tile + 2 + RING
                        split_low(unit + j, j % 2, j % RING)
                first = DOWN_MERGE + 16 * i
                if isinstance(i, int) and i == 0:
                    dve.wait_ge(h_back, 16)
                for d in range(16):
                    hf, k = d // 8, d % 8
                    cols = slice(hf * HALF, (hf + 1) * HALF)
                    dve.wait_ge(down_done, first + d + 1)
                    nc.vector.tensor_tensor(h[:, k, cols], bank[4 + d % 4][:], h[:, k, cols], ALU.add).then_inc(down_added, 1)
                    if last and d:
                        low(2, (d - 1) // 8, (d - 1) % 8)
                if last:
                    low(2, 1, KT - 1)
                for j in range(2):
                    split_low(unit + 10 + j, j % 2, 2 + j)

            merge_step(0)
            with dve.Fori(1, MERGE_STEPS - 1) as i:
                merge_step(i)
            merge_step(MERGE_STEPS - 1, last=True)
            invert(2, 0)
            ffn_step(0, 1)
            with dve.Fori(1, FFN_STEPS - 1) as i:
                ffn_step(i, 1)
            ffn_step(FFN_STEPS - 1, 1, last=True)

        @block.tensor
        def _(pe):
            def product(out, slot, col, moving, first, last):
                hi, lo = moving
                cols = slice(col * P, (col + 1) * P)
                nc.tensor.matmul(out, wh[slot][:, cols], hi, start=first, stop=False)
                nc.tensor.matmul(out, wh[slot][:, cols], lo, start=False, stop=False)
                return nc.tensor.matmul(out, wl[slot][:, cols], hi, start=False, stop=last)

            def normed(k, hf):
                cols = slice(hf * HALF, (hf + 1) * HALF)
                return xh[:, k, cols], xl[:, k, cols]

            def gated(t, hf):
                cols = slice(hf * HALF, (hf + 1) * HALF)
                return gh[:, t, cols], gl[:, t, cols]

            def project(out, slot, hf, norm=None):
                for k in range(KT):
                    if norm is not None:
                        pe.wait_ge(x_low, 16 * norm + 8 * hf + k + 1)
                    last = product(out, slot, k, normed(k, hf), k == 0, k == KT - 1)
                return last

            def sum_squares(norm, hf):
                out = bank[NORM_BANK[norm][hf]][:]
                late = LATE if (norm, hf) == (3, 1) else 0
                pe.wait_ge(made, 2)
                pe.wait_ge(sq_sum, (KT - 1) * (2 * norm + hf + 1) - late)
                last = nc.tensor.matmul(out, ones[:], acc[hf][:], start=True, stop=not late)
                for k in range(KT - late, KT):
                    pe.wait_ge(sq_done, 16 * norm + 8 * hf + k + 1)
                    last = nc.tensor.matmul(out, ones[:], sq[k % 2][:], start=False, stop=k == KT - 1)
                last.then_inc(ssq, 1)

            def distance_biases():
                pe.wait_ge(made, 5)
                pe.wait_ge(tab_in, 32)
                for v, (first, n) in enumerate(((0, 4), (4, 4), (8, 4), (12, 8))):
                    nc.tensor.matmul(bank[4 + v][0:n, 0:VEC], tab[:, first:first + n], hot[:, v, :], start=True, stop=True).then_inc(vec_done, 1)

            def ffn_step(i, f, last=False):
                step = i + FFN_STEPS * f
                unit = FFN_UNITS * i + (FFN2_0 if f else 0)
                first_step = isinstance(i, int) and i == 0
                for t in range(4):
                    tile, hf = t % 2, t // 2
                    if not (first_step and t < 2 and not f):
                        pe.wait_ge(gu_out, 8 * step + 2 * t - 2)
                    if first_step and f and t == 1:
                        pe.wait_ge(rstd_done, 5)
                    norm = 2 * f if first_step and tile == 0 else None
                    for part in range(2):
                        if hf == 0:
                            pe.wait_ge(w_low, unit + 2 * tile + part + 1)
                        done = project(bank[2 * (t % 2) + part][:], 2 * tile + part, hf, norm if part == 0 else None)
                        if first_step and not f and (t, part) in ((1, 0), (2, 1)):
                            pe.wait_ge(vec_out, t)
                            sum_squares(0, t - 1)
                    done.then_inc(gu_done, 1)
                    if first_step and t == 0:
                        if f:
                            sum_squares(2, 1)
                        else:
                            distance_biases()
                first = 16 * step + (DOWN_FFN2 - 16 * FFN_STEPS if f else 0)
                pe.wait_ge(w_low, unit + 6)
                if first_step and not f:
                    pe.wait_ge(root, 2)
                for d in range(16):
                    hf, k = d // 8, d % 8
                    if k == 0:
                        pe.wait_ge(g_low, 4 * step + 2 * hf + 2)
                    if not (first_step and not f and d < 4):
                        pe.wait_ge(down_added, first + d - 3)
                    for t in range(2):
                        done = product(bank[4 + d % 4][:], 4 + t, k, gated(t, hf), t == 0, t == 1)
                    done.then_inc(down_done, 1)
                    if last and d == (12 if f else 15):
                        sum_squares(1 + 2 * f, 0)

            ffn_step(0, 0)
            with pe.Fori(1, FFN_STEPS - 1) as i:
                ffn_step(i, 0)
            ffn_step(FFN_STEPS - 1, 0, last=True)

            tiles = proj_tiles()
            for e in PLAN:
                if e[0] in ("mix", "w", "exp"):
                    continue
                if e[0] == "ssq":
                    sum_squares(1, 1)
                elif e[0] == "job":
                    n, hf = JOBS[e[1]]
                    if hf == 0:
                        pe.wait_ge(w_low, PROJ_0 + n + 1)
                    if e[1] >= 2:
                        pe.wait_ge(job_scaled, e[1] - 1)
                    project(bank[e[1] % 2][:], n % RING, hf, 1 if n == 0 else None).then_inc(job_done, 1)
                elif e[0] == "qk":
                    c = e[1]
                    u, a, j = c // 4, c // 2 % 2, c % 2
                    q_tile, k_tile = tiles.index(("q", u)), tiles.index(("k", min(u, A_UNITS)))
                    q, k = qs[u % 2], ks[min(u, A_UNITS) % 2]
                    part = slice(a * HD, (a + 1) * HD)
                    if c == 0:
                        pe.wait_ge(m_out, HEADS // 2)
                    pe.wait_ge(job_out, JOB_INDEX[(max(q_tile, k_tile), 1)] + 1)
                    for i in range(4):
                        tile = 4 * j + i
                        lo = 0 if has_previous(u, tile) else P
                        if c and i % 2 == 0:
                            pe.wait_ge(max_done, 4 * (c - 1) + 2 * (i // 2) + 2)
                        last = nc.tensor.matmul(bank[2 + i // 2][:, i % 2 * 2 * P + lo:(i % 2 + 1) * 2 * P],
                                                q[part, tile * P:(tile + 1) * P],
                                                k[part, (tile - 1) * P + lo:(tile + 1) * P], start=True, stop=True)
                        if i % 2:
                            last.then_inc(qk_done, 1)
                elif e[0] == "t":
                    c = e[1]
                    u, j = c // 4, c % 2
                    pe.wait_ge(exp_done, c + 1)
                    for i in range(4):
                        if c and i % 2 == 0:
                            pe.wait_ge(t_out[i // 2], c)
                        for b in range(0 if has_previous(u, 4 * j + i) else 1, 2):
                            last = nc.tensor.transpose(bank[4 + i // 2][:, (i % 2 * 2 + b) * P:(i % 2 * 2 + b + 1) * P],
                                                       sp[c % 3][:, i, b * P:(b + 1) * P], ident[:])
                        if i % 2:
                            last.then_inc(t_done, 1)
                elif e[0] == "pv":
                    c = e[1]
                    u, a, j = c // 4, c // 2 % 2, c % 2
                    vu = min(u, A_UNITS)
                    pe.wait_ge(m_out, M_INDEX[("m", "v", vu, 1)] + 1)
                    pe.wait_ge(t_out[0], c + 1)
                    pe.wait_ge(t_out[1], c + 1)
                    if c:
                        pe.wait_ge(pv_out, c)
                    for i in range(4):
                        tile = 4 * j + i
                        start = 0 if has_previous(u, tile) else 1
                        for b in range(start, 2):
                            last = nc.tensor.matmul(bank[6][:, i * HD:(i + 1) * HD], pt[c % 2][:, i, b * P:(b + 1) * P],
                                                    vs[vu % 2][:, tile - 1 + b, a * HD:(a + 1) * HD], start=b == start, stop=b == 1)
                    last.then_inc(pv_done, 1)
                else:
                    m = M_INDEX[e]
                    in_bank = max([n for n in range(m) if misc_bank(n) == misc_bank(m)], default=None)
                    if in_bank is not None:
                        pe.wait_ge(m_out, in_bank + 1)
                    if e[1] == "bias":
                        if e[2] == 0:
                            pe.wait_ge(skew_in, 16)
                            pe.wait_ge(made, 7)
                        last = nc.tensor.matmul(bank[misc_bank(m)][:], flip[:], skew[:, 2 * e[2]:2 * e[2] + 2, :].rearrange("p h k -> p (h k)"),
                                                start=True, stop=True)
                    elif e[1] == "v":
                        u, hf = e[2], e[3]
                        pe.wait_ge(job_out, JOB_INDEX[(tiles.index(("v", u)), 1)] + 1)
                        for i in range(4):
                            last = nc.tensor.transpose(bank[7][:, i * P:(i + 1) * P], vt[:, (4 * hf + i) * P:(4 * hf + i + 1) * P], ident[:])
                    elif e[1] == "o":
                        u, hf = e[2], e[3]
                        pe.wait_ge(pv_out, 4 * u + 3 + hf)
                        for i in range(4):
                            last = nc.tensor.transpose(bank[7][:, i * P:(i + 1) * P], ob[:, 4 * hf + i, :], ident[:])
                    else:
                        _, _, pair, hf, g = e
                        for i in range(4 if g < 2 else 8):
                            b = g if g < 2 else 2 + i // 4
                            if i % 4 == 0:
                                pe.wait_ge(wide_done, 4 * (2 * pair + hf) + b + 1)
                            values = (wide_0 if b % 2 == 0 else wide_1[pair])[:, i % 4, :, :].rearrange("k a d -> k (a d)")
                            if g < 2:
                                out, columns = bank[7][:, i * P:(i + 1) * P], ident[:]
                            else:
                                out = bank[7][:, i * HD:(i + 1) * HD]
                                columns = ident[:].rearrange("k (s j) -> k s j", s=2)[:, :, 32 * hf:32 * hf + 32]
                            last = nc.tensor.matmul(out, values, columns, start=True, stop=True)
                    last.then_inc(m_done, 1)

            def merge_step(i, last=False):
                unit = MERGE_0 + MERGE_UNITS * i
                first_step = isinstance(i, int) and i == 0
                for t in range(4):
                    tile, hf = t // 2, t % 2
                    job = 4 * i + t
                    cols = slice(hf * HALF, (hf + 1) * HALF)
                    for part in range(4):
                        gate = part // 2
                        if hf == 0 and part != 3:
                            pe.wait_ge(w_low, unit + 3 * tile + (0, 2, 1)[part] + 1 if part != 1 else unit + 3 * tile + 3)
                        if first_step and t == 0:
                            if part == 0:
                                pe.wait_ge(job_scaled, 2 * PROJ)
                            elif part == 1:
                                pe.wait_ge(m_out, len(M_EVENTS))
                        else:
                            pe.wait_ge(mul_done, 5 * job - 4 + part)
                        slot = (3 * tile + gate) % RING
                        if part % 2 == 0:
                            done = project(bank[part][:], slot, hf)
                        else:
                            slot = (3 * tile + 2) % RING
                            ys = [(yah[p], yal[p]) for p in range(2)] if gate == 0 else [(ybh[p], ybl[p]) for p in range(B_UNITS)]
                            for p, (hi, lo) in enumerate(ys):
                                done = product(bank[part][:], slot, 2 * gate + p, (hi[:, cols], lo[:, cols]), p == 0, p == len(ys) - 1)
                        done.then_inc(part_done, 1)
                pe.wait_ge(w_low, unit + 8)
                first = DOWN_MERGE + 16 * i
                for d in range(16):
                    hf, k = d // 8, d % 8
                    if k == 0:
                        pe.wait_ge(m_low, 4 * i + 3 + hf)
                    pe.wait_ge(down_added, first + d - 3)
                    for t in range(2):
                        done = product(bank[4 + d % 4][:], 2 + t, k, gated(t, hf), t == 0, t == 1)
                    done.then_inc(down_done, 1)
                    if last and d == 15:
                        sum_squares(2, 0)

            merge_step(0)
            with pe.Fori(1, MERGE_STEPS - 1) as i:
                merge_step(i)
            merge_step(MERGE_STEPS - 1, last=True)
            ffn_step(0, 1)
            with pe.Fori(1, FFN_STEPS - 1) as i:
                ffn_step(i, 1)
            ffn_step(FFN_STEPS - 1, 1, last=True)
            sum_squares(3, 1)


def kernel(x, ffn1_norm, ffn1_w_gate, ffn1_w_up, ffn1_w_down, mix_norm, w_in, b_in, w_branch_a, w_branch_b, w_out,
           sinks, rel_bias, ffn2_norm, ffn2_w_gate, ffn2_w_up, ffn2_w_down, final_norm):
    import concourse.bacc as bacc
    from concourse.bass_utils import run_bass_kernel_spmd

    stream = np.zeros((N_UNITS, P, UNIT), np.float32)
    at = iter(range(N_UNITS))

    def columns(w, cols):
        stream[next(at)] = w[:, cols].reshape(KT, P, P).transpose(1, 0, 2).reshape(P, UNIT)

    def ffn(gate, up, down):
        for i in range(FFN_STEPS):
            for t in (2 * i, 2 * i + 1):
                columns(gate, np.arange(t * P, (t + 1) * P))
                columns(up, np.arange(t * P, (t + 1) * P))
            for t in (2 * i, 2 * i + 1):
                stream[next(at)] = down[t * P:(t + 1) * P, :]

    w = np.asarray(w_in[0])
    b = np.asarray(b_in[0])
    ffn(np.asarray(ffn1_w_gate[0]), np.asarray(ffn1_w_up[0]), np.asarray(ffn1_w_down[0]))
    order = [head_columns(role, u) for role, u in proj_tiles()]
    for cols in order:
        columns(w, cols)
    gates = D_IN - 2 * D_MODEL
    wa, wo = np.asarray(w_branch_a[0]), np.asarray(w_out[0])
    wb = np.asarray(w_branch_b[0]).reshape(2, B_UNITS, HD, D_MODEL).transpose(1, 0, 2, 3).reshape(B_HEADS * HD, D_MODEL)
    for i in range(MERGE_STEPS):
        for t in (2 * i, 2 * i + 1):
            pair = [np.arange(gates + g * D_MODEL + t * P, gates + g * D_MODEL + (t + 1) * P) for g in range(2)]
            order += pair
            for cols in pair:
                columns(w, cols)
            both = np.concatenate([wa, wb])[:, t * P:(t + 1) * P].reshape(6, P, P).transpose(1, 0, 2).reshape(P, 6 * P)
            stream[next(at), :, 0:6 * P] = both
        for t in (2 * i, 2 * i + 1):
            stream[next(at)] = wo[t * P:(t + 1) * P, :]
    ffn(np.asarray(ffn2_w_gate[0]), np.asarray(ffn2_w_up[0]), np.asarray(ffn2_w_down[0]))

    norms = [np.asarray(ffn1_norm[0]), np.asarray(mix_norm[0]), np.asarray(ffn2_norm[0]), np.asarray(final_norm)]
    arrays = {
        "xT": np.ascontiguousarray(np.asarray(x[0]).T),
        "stream": stream,
        "gains": np.ascontiguousarray(np.stack(norms).reshape(4, KT, P).transpose(2, 0, 1)),
        "b_in": np.ascontiguousarray(np.stack([b[c] for c in order]).T),
        "sinks": np.ascontiguousarray(np.asarray(sinks[0])),
        "rel_bias": np.ascontiguousarray(np.asarray(rel_bias)),
        "onehot": distance_onehot(),
    }
    nc = bacc.Bacc("TRN2", target_bir_lowering=False, num_devices=1, dynamic_dma_scratch_size=4096)
    args = [nc.dram_tensor(n, a.shape, mybir.dt.from_np(a.dtype), kind="ExternalInput").ap() for n, a in arrays.items()]
    bias_rows = nc.dram_tensor("bias_rows", (HEADS, VEC), mybir.dt.float32, kind="Internal").ap()
    h_spill = nc.dram_tensor("h_spill", (P, KT, SEQ), mybir.dt.float32, kind="Internal").ap()
    outT = nc.dram_tensor("outT", (D_MODEL, SEQ), mybir.dt.float32, kind="ExternalOutput").ap()
    build(nc, *args, bias_rows, h_spill, outT)
    r = run_bass_kernel_spmd(nc, [arrays], core_ids=[0])
    return np.ascontiguousarray(r.results[0]["outT"].T)[None]
```
